# Optimizing a Trainium2 kernel written in Bass

```python
import jax, jax.numpy as jnp
from jax import lax

D_MODEL = 1024
BATCH = 1
SEQ = 256
DEPTH = 1

GRID_W = 64
CTX_LEN = 256
N_MIXERS = 2
MIXER_NA = 0
MIXER_CONV = 1
N_HEADS = 16
HEAD_DIM = D_MODEL // N_HEADS
WIN_ROWS = 8
WIN_COLS = 16
CONV_WIDTH = 31
N_EXPERTS = 32
TOP_K = 4
D_EXPERT = D_MODEL
SWIGLU_LIMIT = 7.0
SWIGLU_ALPHA = 1.702
EXPERT_BLOCK = 256
NORM_EPS = 1e-6

kernel_name = "hybrid_natten_conformer_moe_diffusion_block"

def rms_norm(x, g):
    xf = x.astype(jnp.float32)
    y = xf * lax.rsqrt(jnp.mean(xf * xf, axis=-1, keepdims=True) + NORM_EPS)
    return (y * g.astype(jnp.float32)).astype(x.dtype)

def layer_norm(x, g, b):
    xf = x.astype(jnp.float32)
    mu = jnp.mean(xf, axis=-1, keepdims=True)
    var = jnp.mean(jnp.square(xf - mu), axis=-1, keepdims=True)
    y = (xf - mu) * lax.rsqrt(var + NORM_EPS)
    return (y * g.astype(jnp.float32) + b.astype(jnp.float32)).astype(x.dtype)

def modulate(h, shift, scale):
    return h * (1 + scale) + shift

def split_heads(t):
    return t.reshape(t.shape[:-1] + (N_HEADS, HEAD_DIM))

def context_feeds_later_layer(i):
    return any(j % N_MIXERS == MIXER_NA for j in range(i + 1, DEPTH))

def dense_attention(q, k, v):
    s = jnp.einsum('bqhd,bkhd->bhqk', q, k).astype(jnp.float32) * (HEAD_DIM ** -0.5)
    p = jax.nn.softmax(s, axis=-1).astype(v.dtype)
    o = jnp.einsum('bhqk,bkhd->bqhd', p, v)
    return o.reshape(o.shape[:2] + (D_MODEL,))

def neighbourhood_attention(q, k, v, k_ctx, v_ctx, rpb):
    b, s = q.shape[0], q.shape[1]
    rows = s // GRID_W
    wr = min(WIN_ROWS, rows)
    n_lat = wr * WIN_COLS
    grid = lambda t: t.reshape(b, rows, GRID_W, N_HEADS, HEAD_DIM)
    qg, kg, vg = grid(q), grid(k), grid(v)
    cols = jnp.arange(GRID_W)
    col_idx = jnp.clip(cols - WIN_COLS // 2, 0, GRID_W - WIN_COLS)[:, None] + jnp.arange(WIN_COLS)[None, :]
    col_off = col_idx - cols[:, None] + (WIN_COLS - 1)
    rpb_f = rpb.astype(jnp.float32)
    scale = HEAD_DIM ** -0.5

    def row_block(r):
        rs = jnp.clip(r - WIN_ROWS // 2, 0, rows - wr)
        qb = lax.dynamic_index_in_dim(qg, r, axis=1, keepdims=False)

        def gather_kv(t):
            t = lax.dynamic_slice_in_dim(t, rs, wr, axis=1)[:, :, col_idx]
            return jnp.moveaxis(t, 2, 1).reshape(b, GRID_W, n_lat, N_HEADS, HEAD_DIM)

        kb, vb = gather_kv(kg), gather_kv(vg)
        row_off = rs + jnp.arange(wr) - r + (WIN_ROWS - 1)
        bias = rpb_f[:, row_off[None, :, None], col_off[:, None, :]].reshape(N_HEADS, GRID_W, n_lat)
        s_lat = jnp.einsum('bqhd,bqkhd->bhqk', qb, kb).astype(jnp.float32) * scale + bias
        s_ctx = jnp.einsum('bqhd,bkhd->bhqk', qb, k_ctx).astype(jnp.float32) * scale
        p = jax.nn.softmax(jnp.concatenate([s_lat, s_ctx], axis=-1), axis=-1).astype(v.dtype)
        return (jnp.einsum('bhqk,bqkhd->bqhd', p[..., :n_lat], vb)
                + jnp.einsum('bhqk,bkhd->bqhd', p[..., n_lat:], v_ctx))

    o = lax.map(row_block, jnp.arange(rows))
    return jnp.moveaxis(o, 0, 1).reshape(b, s, D_MODEL)

def conformer_conv(h, w_pw1, b_pw1, w_dw, b_dw, ln_g, ln_b, w_pw2, b_pw2):
    a = h @ w_pw1 + b_pw1
    u = a[..., :D_MODEL] * jax.nn.sigmoid(a[..., D_MODEL:])
    u = lax.conv_general_dilated(u, w_dw[:, None, :].astype(u.dtype), (1,), [(CONV_WIDTH // 2, CONV_WIDTH // 2)],
                                 dimension_numbers=('NWC', 'WIO', 'NWC'), feature_group_count=D_MODEL) + b_dw
    u = jax.nn.silu(layer_norm(u, ln_g, ln_b))
    return u @ w_pw2 + b_pw2

def clamped_swiglu_expert(xb, w_gu, b_gu, w_down, b_down):
    gu = xb @ w_gu + b_gu
    gate = jnp.minimum(gu[..., :D_EXPERT], SWIGLU_LIMIT)
    up = jnp.clip(gu[..., D_EXPERT:], -SWIGLU_LIMIT, SWIGLU_LIMIT)
    glu = gate * jax.nn.sigmoid(gate * SWIGLU_ALPHA)
    return ((up + 1) * glu) @ w_down + b_down

def moe(h, w_router, b_router, w_gu, b_gu, w_down, b_down):
    shape = h.shape
    x = h.reshape(-1, D_MODEL)
    n_tok = x.shape[0]
    logits = (x @ w_router + b_router).astype(jnp.float32)
    top_val, top_idx = lax.top_k(logits, TOP_K)
    gates = jax.nn.softmax(top_val, axis=-1)
    n_assign = n_tok * TOP_K
    flat_e = top_idx.reshape(-1)
    flat_tok = jnp.repeat(jnp.arange(n_tok), TOP_K)
    order = jnp.argsort(flat_e, stable=True)
    se, stok, sg = flat_e[order], flat_tok[order], gates.reshape(-1)[order]
    counts = jnp.bincount(flat_e, length=N_EXPERTS)
    start = jnp.cumsum(counts) - counts
    pcounts = (counts + EXPERT_BLOCK - 1) // EXPERT_BLOCK * EXPERT_BLOCK
    pend = jnp.cumsum(pcounts)
    pstart = pend - pcounts
    dest = pstart[se] + (jnp.arange(n_assign) - start[se])
    n_blocks = -(-n_assign // EXPERT_BLOCK) + N_EXPERTS
    n_rows = n_blocks * EXPERT_BLOCK
    row_tok = jnp.full((n_rows,), n_tok, jnp.int32).at[dest].set(stok)
    row_gate = jnp.zeros((n_rows,), x.dtype).at[dest].set(sg.astype(x.dtype))
    blk_e = jnp.minimum(jnp.searchsorted(pend, jnp.arange(n_blocks) * EXPERT_BLOCK, side='right'), N_EXPERTS - 1)
    x_pad = jnp.concatenate([x, jnp.zeros((1, D_MODEL), x.dtype)], axis=0)

    def expert_block(args):
        tok, e = args
        return clamped_swiglu_expert(x_pad[tok], w_gu[e], b_gu[e], w_down[e], b_down[e])

    y = lax.map(expert_block, (row_tok.reshape(n_blocks, EXPERT_BLOCK), blk_e))
    y = y.reshape(n_rows, D_MODEL) * row_gate[:, None]
    out = jnp.zeros((n_tok + 1, D_MODEL), y.dtype).at[row_tok].add(y)[:n_tok]
    return out.reshape(shape)

def setup_inputs(seed: int = 0) -> dict:
    key = jax.random.key(seed)
    ks = jax.random.split(key, 24)
    d, e, f = D_MODEL, N_EXPERTS, D_EXPERT
    n_na = len(range(MIXER_NA, DEPTH, N_MIXERS))
    n_conv = len(range(MIXER_CONV, DEPTH, N_MIXERS))
    nrm = lambda k, shp, s: jax.random.normal(k, shp, jnp.float32) * s
    return {
        'x': nrm(ks[0], (BATCH, SEQ, d), 1.0),
        'c': nrm(ks[1], (BATCH, d), 1.0),
        'ctx': nrm(ks[2], (BATCH, CTX_LEN, d), 1.0),
        'c_ctx': nrm(ks[3], (d,), 1.0),
        'w_ada': nrm(ks[4], (DEPTH, d, 6 * d), 0.5 * d ** -0.5),
        'b_ada': nrm(ks[5], (DEPTH, 6 * d), 0.01),
        'norm_g': 1.0 + nrm(ks[6], (DEPTH, 4, d), 0.1),
        'w_qkv': nrm(ks[7], (n_na, d, 3 * d), d ** -0.5),
        'w_o': nrm(ks[8], (n_na, d, d), d ** -0.5),
        'rpb': nrm(ks[9], (n_na, N_HEADS, 2 * WIN_ROWS - 1, 2 * WIN_COLS - 1), 0.1),
        'w_pw1': nrm(ks[10], (n_conv, d, 2 * d), d ** -0.5),
        'b_pw1': nrm(ks[11], (n_conv, 2 * d), 0.01),
        'w_dw': nrm(ks[12], (n_conv, CONV_WIDTH, d), CONV_WIDTH ** -0.5),
        'b_dw': nrm(ks[13], (n_conv, d), 0.01),
        'cn_g': 1.0 + nrm(ks[14], (n_conv, d), 0.1),
        'cn_b': nrm(ks[15], (n_conv, d), 0.01),
        'w_pw2': nrm(ks[16], (n_conv, d, d), d ** -0.5),
        'b_pw2': nrm(ks[17], (n_conv, d), 0.01),
        'w_router': nrm(ks[18], (DEPTH, d, e), d ** -0.5),
        'b_router': nrm(ks[19], (DEPTH, e), 0.01),
        'w_gu': nrm(ks[20], (DEPTH, e, d, 2 * f), d ** -0.5),
        'b_gu': nrm(ks[21], (DEPTH, e, 2 * f), 0.01),
        'w_down': nrm(ks[22], (DEPTH, e, f, d), f ** -0.5),
        'b_down': nrm(ks[23], (DEPTH, e, d), 0.01),
    }

def reference(x, c, ctx, c_ctx, w_ada, b_ada, norm_g, w_qkv, w_o, rpb, w_pw1, b_pw1, w_dw, b_dw,
              cn_g, cn_b, w_pw2, b_pw2, w_router, b_router, w_gu, b_gu, w_down, b_down):
    silu_c = jax.nn.silu(c)
    silu_cc = jax.nn.silu(c_ctx)
    for i in range(DEPTH):
        kind, j = i % N_MIXERS, i // N_MIXERS
        ctx_live = context_feeds_later_layer(i)
        sh1, sc1, g1, sh2, sc2, g2 = jnp.split((silu_c @ w_ada[i] + b_ada[i])[:, None, :], 6, axis=-1)
        if kind == MIXER_NA or ctx_live:
            csh1, csc1, cg1, csh2, csc2, cg2 = jnp.split(silu_cc @ w_ada[i] + b_ada[i], 6)
            hc = modulate(rms_norm(ctx, norm_g[i, 0]), csh1, csc1)
        h = modulate(rms_norm(x, norm_g[i, 0]), sh1, sc1)
        if kind == MIXER_NA:
            w = w_qkv[j]
            q, k, v = [split_heads(t) for t in jnp.split(h @ w, 3, axis=-1)]
            kc, vc = [split_heads(t) for t in jnp.split(hc @ w[:, D_MODEL:], 2, axis=-1)]
            y = neighbourhood_attention(q, k, v, kc, vc, rpb[j]) @ w_o[j]
            if ctx_live:
                yc = dense_attention(split_heads(hc @ w[:, :D_MODEL]), kc, vc) @ w_o[j]
        else:
            conv_w = (w_pw1[j], b_pw1[j], w_dw[j], b_dw[j], cn_g[j], cn_b[j], w_pw2[j], b_pw2[j])
            y = conformer_conv(h, *conv_w)
            if ctx_live:
                yc = conformer_conv(hc, *conv_w)
        moe_w = (w_router[i], b_router[i], w_gu[i], b_gu[i], w_down[i], b_down[i])
        x = x + g1 * rms_norm(y, norm_g[i, 1])
        x = x + g2 * rms_norm(moe(modulate(rms_norm(x, norm_g[i, 2]), sh2, sc2), *moe_w), norm_g[i, 3])
        if ctx_live:
            ctx = ctx + cg1 * rms_norm(yc, norm_g[i, 1])
            ctx = ctx + cg2 * rms_norm(moe(modulate(rms_norm(ctx, norm_g[i, 2]), csh2, csc2), *moe_w), norm_g[i, 3])
    return x


_drawn_inputs = setup_inputs


def setup_inputs(seed=0):
    import zlib

    import numpy as np

    out = dict(_drawn_inputs(seed))
    spreads = {}
    factors = {'rpb': 3.64, 'b_router': 2.826, 'b_gu': 8.0, 'b_down': 8.0}
    for name, (base, spread) in spreads.items():
        noise = np.random.default_rng([zlib.crc32(name.encode()), seed]).standard_normal(out[name].shape)
        drawn = base * np.exp(spread * noise) if base else spread * noise
        out[name] = __import__('jax').numpy.asarray(drawn.astype(out[name].dtype))
    for name, factor in factors.items():
        out[name] = (out[name] * factor).astype(out[name].dtype)
    return out
```

```python
from contextlib import ExitStack

import concourse.bass as bass
from concourse import mybir

F32 = mybir.dt.float32
I32 = mybir.dt.int32
U32 = mybir.dt.uint32
ALU = mybir.AluOpType
ACT = mybir.ActivationFunctionType
AX = mybir.AxisListType

P = 128
D = 1024
KC = D // P
SEQ = 256
CTX = 256
TT = SEQ // P
TA = (SEQ + CTX) // P
KEYS = SEQ + CTX
HEADS = 16
HD = D // HEADS
GRID_W = 64
WIN_ROWS, WIN_COLS = 8, 16
RPB_R, RPB_C = 2 * WIN_ROWS - 1, 2 * WIN_COLS - 1
ROWS = SEQ // GRID_W
BROWS = ROWS + 2
E = 32
TOPK = 4
EPS = 1e-6
LIMIT = 7.0
ALPHA = 1.702
MASKED = -1e30
SLOTS = 64
BANK = 512
GU = 2 * D
UC = D // P
RING = 4


def build(nc, x, c_cols, ctx, w_ada, b_ada_cols, b_ada, norm_cols, norm_g, w_qkv, w_o, rpb,
          w_router, b_router, w_gu, b_gu_cols, w_down, b_down, out):
    with ExitStack() as stack:
        def sb(name, shape, dt=F32):
            return stack.enter_context(nc.sbuf_tensor(name, shape, dt))

        def sem(name):
            return stack.enter_context(nc.semaphore(name))

        psum = stack.enter_context(nc.psum_tensor("psum", [P, 8, BANK], F32))

        warena = sb("warena", [P, 3 * KC * D])
        gu_slot = [warena[:, k * GU:(k + 1) * GU] for k in range(KC)]
        dn0 = KC * GU
        down_slot = [warena[:, dn0 + f * D:dn0 + (f + 1) * D] for f in range(KC)]
        ada_slot = gu_slot
        q_words = KC * BANK
        qkv_at = [dn0, dn0 + q_words] + [b * q_words for b in range(4)]
        qkv_blk = [warena[:, a:a + q_words].rearrange("p (k n) -> p k n", k=KC) for a in qkv_at]
        bias0 = 3 * KC * D - HEADS * BROWS * GRID_W
        bias = warena[:, bias0:].rearrange("p (h r w) -> p h r w", h=HEADS, r=BROWS)
        bada_rows = warena[:, bias0 - D:bias0]
        wo_sb = warena[:, 0:KC * D].rearrange("p (k n) -> p k n", k=KC)

        parena = sb("parena", [P, 14 * D])
        hT = parena[:, 0:4 * D].rearrange("p (k n) -> p k n", k=KC)
        xn = parena[:, 4 * D:8 * D].rearrange("p (t n) -> p t n", t=TA)
        kT = parena[:, 4 * D:8 * D].rearrange("p (k n) -> p k n", k=KC)
        v_sb = parena[:, 8 * D:12 * D].rearrange("p (t n) -> p t n", t=TA)
        qT = parena[:, 12 * D:14 * D].rearrange("p (k n) -> p k n", k=KC)
        o_sb = parena[:, 0:2 * D].rearrange("p (t n) -> p t n", t=TT)
        oT = parena[:, 2 * D:4 * D].rearrange("p (k n) -> p k n", k=KC)
        acc = parena[:, 4 * D:6 * D].rearrange("p (t n) -> p t n", t=TT)
        h2T = parena[:, 6 * D:8 * D].rearrange("p (k n) -> p k n", k=KC)
        square = parena[:, 8 * D:9 * D]
        scaled = parena[:, 9 * D:11 * D].rearrange("p (t n) -> p t n", t=TT)

        bd_sb = parena[0:E, 11 * D:12 * D]
        eq, geq = (parena[:, 12 * D + i * 256:12 * D + (i + 1) * 256]
                   .rearrange("p (t k e) -> p t k e", t=TT, k=TOPK) for i in range(2))

        x_sb = sb("x_sb", [P, TT, D])
        h2 = sb("h2", [P, TT, D])
        ctx_sb = h2
        ring2 = h2[:].rearrange("p t n -> p (t n)")
        g2_row = sb("g2_row", [P, D])

        work = sb("work", [P, 6 * D])
        g1_row, sh2_row, a2_row = (work[:, i * D:(i + 1) * D] for i in range(3))
        ada_acc = work[:, 3 * D:4 * D]
        ring = [ring2[:, 0:D], ring2[:, D:2 * D], work[:, 4 * D:5 * D], work[:, 5 * D:6 * D]]
        probs = [work[:, (3 + i) * D:(4 + i) * D].rearrange("p (t n) -> p t n", t=TT) for i in range(2)]
        probsT = work[:, 5 * D:6 * D].rearrange("p (k n) -> p k n", k=TA)
        W8 = UC * SLOTS

        def work8(i):
            return work[:, i * W8:(i + 1) * W8].rearrange("p (k s) -> p k s", k=UC)
        y_sb = work[:, 0:BANK]
        xgT, gate_sb, up_sb, sig_sb, hid_sb, yT_sb = (work8(2 + i) for i in range(6))
        selT = work[:, 8 * W8:8 * W8 + SEQ]
        sel = work[:, 9 * W8:9 * W8 + TT * 2 * SLOTS].rearrange("p (t c s) -> p t c s", t=TT, c=2)
        gate_slot = work[:, 10 * W8:10 * W8 + 1]

        bgu = sb("bgu", [P, E, 2 * UC])
        wr_sb = sb("wr_sb", [P, KC, E])
        br_sb = sb("br_sb", [P, E])
        ident = sb("ident", [P, P])
        flip = sb("flip", [P, P])
        before = sb("before", [P, P])
        ones = sb("ones", [P, P])
        slot_no = sb("slot_no", [P, SEQ])
        c_sb = sb("c_sb", [P, KC, 2])
        csig = sb("csig", [P, KC, 2])
        silu = sb("silu", [P, KC, 2])
        bac = sb("bac", [P, 2 * KC])
        ng0 = sb("ng0", [P, KC])
        ada = sb("ada", [P, 2 * KC, 2])
        a1 = sb("a1", [P, KC, 2])
        ss = sb("ss", [P, 12])
        var = sb("var", [P, 12])
        std = sb("std", [P, 12])
        rstd = sb("rstd", [P, 12])
        negmax = sb("negmax", [P, HEADS, TT])
        psumexp = sb("psumexp", [P, HEADS, TT])
        rsum = sb("rsum", [P, HEADS, TT])
        logits = sb("logits", [P, TT, E])
        top8 = sb("top8", [P, TT, 8])
        idx8 = sb("idx8", [P, TT, 8], U32)
        idxf = sb("idxf", [P, TT, 8])
        ntop = sb("ntop", [P, TT])
        e4 = sb("e4", [P, TT, TOPK])
        e4s = sb("e4s", [P, TT])
        e4r = sb("e4r", [P, TT])
        g4 = sb("g4", [P, TT, TOPK])
        member = sb("member", [P, TT, E])
        gates = sb("gates", [P, TT, E])
        gatesT = sb("gatesT", [E, SEQ])
        pos = sb("pos", [P, TT, E])
        nblk = sb("nblk", [1, E])
        one_row = sb("one_row", [1, E])
        cum = sb("cum", [1, E + 1])
        first_block = sb("first_block", [1, E + 1], I32)

        x_in, ctx_in, consts_in, tables_in, rows_in, bias_in, wo_in, out_done = (
            sem(n) for n in ("x_in", "ctx_in", "consts_in", "tables_in", "rows_in", "bias_in", "wo_in", "out_done"))
        ada_in = [sem(f"ada_in{k}") for k in range(KC)]
        qkv_in = [sem(f"qkv_in{b}") for b in range(6)]
        ring_in = [sem(f"ring_in{r}") for r in range(RING)]
        bada_in, bdown_in = sem("bada_in"), sem("bdown_in")
        const_ready, bias_masked = sem("const_ready"), sem("bias_masked")
        csig_ready, silu_ready = sem("csig_ready"), sem("silu_ready")
        squares, vars_ready, std_ready, rstd_ready, xn_ready = (
            sem(n) for n in ("squares", "vars_ready", "std_ready", "rstd_ready", "xn_ready"))
        ada_used, ada_ready, a1_ready = sem("ada_used"), sem("ada_ready"), sem("a1_ready")
        xT_ps, hT_dve, hT_act = sem("xT_ps"), sem("hT_dve"), sem("hT_act")
        proj_ps, proj_sb = sem("proj_ps"), sem("proj_sb")
        ada_step, ada_sum_ps, rows_ready = sem("ada_step"), sem("ada_sum_ps"), sem("rows_ready")
        scores_ps, negmax_ready, probs_ready = sem("scores_ps"), sem("negmax_ready"), sem("probs_ready")
        probsT_ps, probsT_sb, pv_ps, rsum_ready, o_ready = (
            sem(n) for n in ("probsT_ps", "probsT_sb", "pv_ps", "rsum_ready", "o_ready"))
        oT_ps, oT_dve, oT_act, attn_out_ps = sem("oT_ps"), sem("oT_dve"), sem("oT_act"), sem("attn_out_ps")
        res_step, x1_ready, h2_ready = sem("res_step"), sem("x1_ready"), sem("h2_ready")
        h2T_ps, h2T_dve, h2T_act, logits_ps = sem("h2T_ps"), sem("h2T_dve"), sem("h2T_act"), sem("logits_ps")
        route_step = sem("route_step")
        route, top_exp, member_ready, gates_ready, pos_ps = (
            sem(n) for n in ("route", "top_exp", "member_ready", "gates_ready", "pos_ps"))
        gatesT_ps, gatesT_sb, bdown_ps, blocks_ready = (
            sem(n) for n in ("gatesT_ps", "gatesT_sb", "bdown_ps", "blocks_ready"))
        gu_in = [sem(f"gu_in{k}") for k in range(KC)]
        down_in = [sem(f"down_in{k}") for k in range(KC // 2)]
        slots_used, sel_ready, selT_ps, selT_sb = (
            sem(n) for n in ("slots_used", "sel_ready", "selT_ps", "selT_sb"))
        xg_ps, xg_sb, gu_ps, swiglu, sig_ready = (
            sem(n) for n in ("xg_ps", "xg_sb", "gu_ps", "swiglu", "sig_ready"))
        yT_ps, yT_ready, y_ps, y_ready, comb_ps, comb_taken = (
            sem(n) for n in ("yT_ps", "yT_ready", "y_ps", "y_ready", "comb_ps", "comb_taken"))
        fin_step, fin_ready = sem("fin_step"), sem("fin_ready")

        block = stack.enter_context(nc.Block())
        N_CONST = 9
        USES = KC + KC // 2
        COUNTED = USES - 2
        MISC, GATE, UP, YB, COMB, SELB = 0, 1, 2, 3, 5, 7

        def expert_slot_dma(sp, s, e):
            if s < KC:
                src = w_gu[bass.ds(e, 1), s * P:(s + 1) * P, :].rearrange("o p n -> (o p) n")
                sp.dma_start(gu_slot[s], src).then_inc(gu_in[s], 16)
            else:
                f = s - KC
                src = w_down[bass.ds(e, 1), 2 * f * P:2 * (f + 1) * P, :].rearrange("o (c p) n -> (o p) c n", c=2)
                dst = warena[:, dn0 + 2 * f * D:dn0 + 2 * (f + 1) * D].rearrange("p (c n) -> p c n", c=2)
                sp.dma_start(dst, src).then_inc(down_in[f], 16)

        @block.sync
        def _(sp):
            sp.dma_start(c_sb[:], c_cols).then_inc(consts_in, 16)
            sp.dma_start(bac[:], b_ada_cols).then_inc(consts_in, 16)
            sp.dma_start(ng0[:], norm_cols).then_inc(consts_in, 16)
            sp.dma_start(x_sb[:], x[0].rearrange("(t p) n -> p t n", p=P)).then_inc(x_in, 16)
            sp.dma_start(ctx_sb[:], ctx[0].rearrange("(t p) n -> p t n", p=P)).then_inc(ctx_in, 16)
            for k in range(KC):
                sp.dma_start(ada_slot[k], w_ada[0, k * P:(k + 1) * P, 0:2 * D]).then_inc(ada_in[k], 16)
            wq = w_qkv[0].rearrange("(k p) n -> p k n", p=P)
            for b in range(6):
                if b >= 2:
                    sp.wait_ge(ada_used, 2 * (b - 1))
                sp.dma_start(qkv_blk[b], wq[:, :, b * BANK:(b + 1) * BANK]).then_inc(qkv_in[b], 16)
            sp.wait_ge(proj_ps, 8)
            for i in range(4):
                sp.dma_start(bada_rows[32 * i:32 * i + 1, :], b_ada[0:1, (2 + i) * D:(3 + i) * D]).then_inc(bada_in, 16)
            for a in range(2):
                for r in range(BROWS):
                    row = WIN_ROWS - 1 - 2 - a + r
                    src = bass.AP(tensor=rpb.tensor, offset=row * RPB_C + WIN_COLS - 1 - (GRID_W - 1),
                                  ap=[[1, GRID_W], [RPB_R * RPB_C, HEADS], [1, GRID_W]])
                    sp.dma_start(bias[GRID_W * a:GRID_W * (a + 1), :, r, :], src).then_inc(bias_in, 16)
            sp.dma_start(bgu[:], b_gu_cols).then_inc(tables_in, 16)
            sp.dma_start(wr_sb[:], w_router[0].rearrange("(k p) e -> p k e", p=P)).then_inc(tables_in, 16)
            sp.dma_start(br_sb[:], b_router.to_broadcast([P, E])).then_inc(tables_in, 16)
            sp.wait_ge(proj_ps, 16)
            sp.dma_start(wo_sb, w_o[0].rearrange("(k p) n -> p k n", p=P)).then_inc(wo_in, 16)
            sp.wait_ge(proj_ps, 24)
            for s in range(4, KC):
                expert_slot_dma(sp, s, 0)
            sp.wait_ge(scores_ps, HEADS)
            sp.wait_ge(rows_ready, 4)
            for s in range(KC, USES):
                expert_slot_dma(sp, s, 0)
            sp.wait_ge(attn_out_ps, TT)
            sp.dma_start(bd_sb, b_down[0]).then_inc(bdown_in, 16)
            for s in range(4):
                expert_slot_dma(sp, s, 0)
            sp.wait_ge(blocks_ready, 1)
            with sp.Fori(1, E) as e:
                done = sp.value_load(first_block[0:1, bass.ds(e, 1)], min_val=1, max_val=4 * E)
                for s in range(USES):
                    if s == KC - 1:
                        sp.wait_ge(gu_ps, 2 * done)
                    elif s == USES - 1:
                        sp.wait_ge(yT_ps, done)
                    else:
                        sp.wait_ge(slots_used, COUNTED * done + (s + 1 if s < KC else s))
                    expert_slot_dma(sp, s, e)
            for t in range(TT):
                sp.wait_ge(fin_ready, t + 1)
                sp.dma_start(out[0, t * P:(t + 1) * P, :], h2[:, t, :]).then_inc(out_done, 16)
            sp.wait_ge(out_done, 16 * TT)

        @block.gpsimd
        def _(pool):
            made = 0

            def make(ins):
                nonlocal made
                made += 1
                ins.then_inc(const_ready, 1)
                pool.wait_ge(const_ready, made)

            make(pool.memset(ident[:], 0.0))
            make(pool.memset(flip[:], 0.0))
            make(pool.memset(before[:], 1.0))
            make(pool.memset(ones[:], 1.0))
            make(pool.affine_select(out=ident[:], in_=ident[:], compare_op=ALU.not_equal, fill=1.0, base=0,
                                    pattern=[[-1, P]], channel_multiplier=1))
            for a in range(2):
                blk = flip[GRID_W * a:GRID_W * (a + 1), GRID_W * a:GRID_W * (a + 1)]
                make(pool.affine_select(out=blk, in_=blk, compare_op=ALU.not_equal, fill=1.0, base=-(GRID_W - 1),
                                        pattern=[[1, GRID_W]], channel_multiplier=1))
            make(pool.affine_select(out=before[:], in_=before[:], compare_op=ALU.is_gt, fill=0.0, base=0,
                                    pattern=[[1, P]], channel_multiplier=-1))
            make(pool.iota(slot_no[:], pattern=[[1, SEQ]], base=0, channel_multiplier=0,
                           allow_small_or_imprecise_dtypes=True))
            for i, row in ((1, g1_row), (2, a2_row), (3, g2_row[:])):
                pool.dma_start(row, norm_g[0, i:i + 1, :].to_broadcast([P, D])).then_inc(rows_in, 16)
            for i in range(4 * KC):
                cb, k = i // KC, i % KC
                if i == 0:
                    pool.wait_ge(xn_ready, TA)
                if i >= RING:
                    last = i - RING
                    pool.wait_ge(ada_step, (KC + 1) * (last // KC) + last % KC + 1)
                pool.dma_start(ring[i % RING], w_ada[0, k * P:(k + 1) * P, (2 + cb) * D:(3 + cb) * D]) \
                    .then_inc(ring_in[i % RING], 16)
            pool.wait_ge(bias_in, 16 * 2 * BROWS)
            for a in range(2):
                tab = bias[GRID_W * a:GRID_W * (a + 1)].rearrange("p h r w -> p (h r) w")
                lo = tab[:, :, 0:GRID_W - WIN_COLS]
                hi = tab[:, :, WIN_COLS:GRID_W]
                n = GRID_W - WIN_COLS
                pool.affine_select(out=lo, in_=lo, compare_op=ALU.is_ge, fill=MASKED,
                                   base=WIN_COLS // 2 - (GRID_W - 1), pattern=[[0, HEADS * BROWS], [1, n]],
                                   channel_multiplier=1).then_inc(bias_masked, 1)
                pool.wait_ge(bias_masked, 2 * a + 1)
                pool.affine_select(out=hi, in_=hi, compare_op=ALU.is_ge, fill=MASKED,
                                   base=GRID_W - 1 + WIN_COLS // 2 - 1 - WIN_COLS,
                                   pattern=[[0, HEADS * BROWS], [-1, n]],
                                   channel_multiplier=-1).then_inc(bias_masked, 1)
                pool.wait_ge(bias_masked, 2 * a + 2)

        @block.tensor
        def _(pe):
            pe.wait_ge(const_ready, N_CONST)
            pe.wait_ge(silu_ready, 1)
            adaT = psum[:, 4, 0:4 * KC].rearrange("p (m v) -> p m v", v=2)
            for k in range(KC):
                pe.wait_ge(ada_in[k], 16)
                for m in range(2 * KC):
                    mm = pe.matmul(adaT[:, m, :], ada_slot[k][:, m * P:(m + 1) * P], silu[:, k, :],
                                   start=(k == 0 and m == 0), stop=(k == KC - 1), skip_group_check=True)
                mm.then_inc(ada_used, 1)
            pe.wait_ge(xn_ready, TA)
            for k in range(KC):
                if k >= 4:
                    pe.wait_ge(hT_dve if k % 2 == 0 else hT_act, k // 2 - 1)
                for t in range(TA):
                    mm = pe.transpose(psum[:, k % 4, t * P:(t + 1) * P], xn[:, t, k * P:(k + 1) * P], ident[:])
                mm.then_inc(xT_ps, 1)

            def ada_sum(cb):
                pe.wait_ge(ada_step, (KC + 1) * (cb + 1))
                if cb >= 1:
                    pe.wait_ge(rows_ready, cb)
                for h in range(2):
                    mm = pe.matmul(psum[:, 6 + h, :], ones[:], ada_acc[:, h * BANK:(h + 1) * BANK],
                                   start=True, stop=True)
                mm.then_inc(ada_sum_ps, 1)

            pe.wait_ge(hT_dve, KC // 2)
            pe.wait_ge(hT_act, KC // 2)
            for n in range(24):
                part, i = n // 8, n % 8
                blk = n // 4
                if n % 4 == 0:
                    pe.wait_ge(qkv_in[blk], 16)
                if n >= 4:
                    pe.wait_ge(proj_sb, n - 3)
                w = qkv_blk[blk]
                for k in range(KC):
                    if part < 2:
                        j = n % 4
                        width = SEQ if part == 0 else KEYS
                        mm = pe.matmul(psum[:, n % 4, 0:width], w[:, k, j * P:(j + 1) * P], hT[:, k, 0:width],
                                       start=(k == 0), stop=(k == KC - 1))
                    else:
                        t = n % 4
                        mm = pe.matmul(psum[:, n % 4, :], hT[:, k, t * P:(t + 1) * P], w[:, k, :],
                                       start=(k == 0), stop=(k == KC - 1))
                mm.then_inc(proj_ps, 1)
                if n in (13, 16, 19, 22):
                    ada_sum((13, 16, 19, 22).index(n))

            def scores(h):
                j, r = h // 2, HD * (h % 2)
                if h < 2:
                    pe.wait_ge(proj_sb, 24)
                    pe.wait_ge(bias_masked, 4)
                else:
                    pe.wait_ge(probs_ready, 2 * (h - 1))
                for t in range(TT):
                    s = psum[:, 2 * (h % 2) + t, :]
                    pe.matmul(s[:, 0:KEYS], qT[r:r + HD, j, t * P:(t + 1) * P], kT[r:r + HD, j, :],
                              start=True, stop=False)
                    mm = pe.matmul(s[:, 0:SEQ], flip[:],
                                   bias[:, h, 2 - 2 * t:2 - 2 * t + ROWS, :].rearrange("p r w -> p (r w)"),
                                   start=False, stop=True)
                mm.then_inc(scores_ps, 1)

            def turn_probs(h):
                pe.wait_ge(probs_ready, 2 * (h + 1))
                if h >= 1:
                    pe.wait_ge(probsT_sb, h)
                for k in range(TA):
                    for t in range(TT):
                        o = (k % 2) * SEQ + t * P
                        mm = pe.transpose(psum[:, 4 + k // 2, o:o + P], probs[h % 2][:, t, k * P:(k + 1) * P], ident[:])
                mm.then_inc(probsT_ps, 1)

            def values(h):
                pe.wait_ge(probsT_sb, h + 1)
                if h < 2:
                    pe.wait_ge(rows_ready, 4)
                else:
                    pe.wait_ge(o_ready, h - 1)
                for t in range(TT):
                    for k in range(TA):
                        mm = pe.matmul(psum[:, 6 + h % 2, t * HD:(t + 1) * HD], probsT[:, k, t * P:(t + 1) * P],
                                       v_sb[:, k, h * HD:(h + 1) * HD], start=(k == 0), stop=(k == TA - 1))
                mm.then_inc(pv_ps, 1)

            for i in range(HEADS + 2):
                if i < HEADS:
                    scores(i)
                if 1 <= i <= HEADS:
                    turn_probs(i - 1)
                if i >= 2:
                    values(i - 2)

            pe.wait_ge(o_ready, HEADS)
            for j in range(KC):
                if j >= 4:
                    pe.wait_ge(oT_dve if j % 2 == 0 else oT_act, j // 2 - 1)
                for t in range(TT):
                    mm = pe.transpose(psum[:, j % 4, t * P:(t + 1) * P], o_sb[:, t, j * P:(j + 1) * P], ident[:])
                mm.then_inc(oT_ps, 1)
            pe.wait_ge(oT_dve, KC // 2)
            pe.wait_ge(oT_act, KC // 2)
            pe.wait_ge(wo_in, 16)
            for t in range(TT):
                for h in range(2):
                    for j in range(KC):
                        mm = pe.matmul(psum[:, 4 + 2 * t + h, :], oT[:, j, t * P:(t + 1) * P],
                                       wo_sb[:, j, h * BANK:(h + 1) * BANK], start=(j == 0), stop=(j == KC - 1))
                mm.then_inc(attn_out_ps, 1)

            pe.wait_ge(h2_ready, TT)
            for k in range(KC):
                if k >= 4:
                    pe.wait_ge(h2T_dve if k % 2 == 0 else h2T_act, k // 2 - 1)
                for t in range(TT):
                    mm = pe.transpose(psum[:, k % 4, t * P:(t + 1) * P], h2[:, t, k * P:(k + 1) * P], ident[:])
                mm.then_inc(h2T_ps, 1)
            pe.wait_ge(h2T_dve, KC // 2)
            pe.wait_ge(h2T_act, KC // 2)
            pe.wait_ge(tables_in, 16 * 3)
            for t in range(TT):
                for k in range(KC):
                    mm = pe.matmul(psum[:, 4, t * E:(t + 1) * E], h2T[:, k, t * P:(t + 1) * P], wr_sb[:, k, :],
                                   start=(k == 0), stop=(k == KC - 1))
            mm.then_inc(logits_ps, 1)
            pe.wait_ge(member_ready, TT)
            pe.matmul(psum[:, 5, 0:E], before[:], member[:, 0, :], start=True, stop=True)
            pe.matmul(psum[:, 5, E:2 * E], ones[:], member[:, 0, :], start=True, stop=False)
            pe.matmul(psum[:, 5, E:2 * E], before[:], member[:, 1, :], start=False, stop=True)
            pe.matmul(psum[:, 5, 2 * E:3 * E], ones[:], member[:, 0, :], start=True, stop=False)
            pe.matmul(psum[:, 5, 2 * E:3 * E], ones[:], member[:, 1, :], start=False, stop=True).then_inc(pos_ps, 1)
            pe.wait_ge(gates_ready, TT)
            for t in range(TT):
                mm = pe.transpose(psum[0:E, 6, t * P:(t + 1) * P], gates[:, t, :], ident[:])
            mm.then_inc(gatesT_ps, 1)
            pe.wait_ge(gatesT_sb, 1)
            pe.wait_ge(bdown_in, 16)
            for t in range(TT):
                for h in range(2):
                    mm = pe.matmul(psum[:, 2 * t + h, :], gatesT[:, t * P:(t + 1) * P],
                                   bd_sb[:, h * BANK:(h + 1) * BANK], start=True, stop=True)
            mm.then_inc(bdown_ps, 1)

            def turn_y(g):
                pe.wait_ge(yT_ready, g + 1)
                pe.wait_ge(y_ready, g + 1)
                for j in range(KC // 2):
                    mm = pe.transpose(psum[:, YB, j * P:(j + 1) * P],
                                      yT_sb[:, 2 * j:2 * j + 2, :].rearrange("p k s -> p (k s)"), ident[:])
                mm.then_inc(y_ps, 1)

            def combine(g, t):
                if t == 0:
                    pe.wait_ge(y_ready, g + 2)
                    pe.wait_ge(selT_sb, 2 * g + 2)
                for h in range(2):
                    n = 2 * t + h
                    pe.wait_ge(comb_taken, 4 * g + n + 3)
                    half = slice(h * SLOTS, (h + 1) * SLOTS)
                    pe.matmul(psum[:, COMB + h, :], selT[half, t * P:(t + 1) * P], y_sb[half, :],
                              start=True, stop=True).then_inc(comb_ps, 1)

            pe.wait_ge(blocks_ready, 1)
            pe.wait_ge(comb_taken, 4)
            with pe.Fori(0, E) as e:
                g_first = pe.value_load(first_block[0:1, bass.ds(e, 1)], min_val=0, max_val=4 * E)
                g_end = pe.value_load(first_block[0:1, bass.ds(e + 1, 1)], min_val=1, max_val=4 * E)
                with pe.Fori(g_first, g_end) as g:
                    pe.wait_ge(sel_ready, g + 1)
                    pe.wait_ge(selT_sb, 2 * g + 2)
                    for t in range(TT):
                        pe.transpose(psum[:, SELB, t * P:(t + 1) * P], sel[:, t].rearrange("p c s -> p (c s)"), ident[:])
                    for t in range(TT):
                        mm = pe.matmul(psum[:, SELB, SEQ:SEQ + 1], sel[:, t].rearrange("p c s -> p (c s)"), gates[:, t, bass.ds(e, 1)],
                                       start=(t == 0), stop=(t == TT - 1))
                    mm.then_inc(selT_ps, 1)
                    pe.wait_ge(yT_ready, g + 1)
                    for k in range(KC):
                        for t in range(TT):
                            mm = pe.matmul(psum[:, MISC, k * SLOTS:(k + 1) * SLOTS], h2[:, t, k * P:(k + 1) * P],
                                           sel[:, t, 0, :], start=(t == 0), stop=(t == TT - 1))
                    mm.then_inc(xg_ps, 1)
                    turn_y(g)
                    pe.wait_ge(xg_sb, g + 1)
                    for k in range(KC):
                        pe.wait_ge(gu_in[k], 16 * e + 16)
                        for m in range(2 * UC):
                            b = GATE + m // UC
                            mm = pe.matmul(psum[:, b, (m % UC) * SLOTS:(m % UC + 1) * SLOTS],
                                           gu_slot[k][:, m * P:(m + 1) * P], xgT[:, k, :],
                                           start=(k == 0 and m % UC == 0), stop=(k == KC - 1), skip_group_check=True)
                            if k == KC - 1 and m == UC - 1:
                                mm.then_inc(gu_ps, 1)
                        if k < KC - 1:
                            mm.then_inc(slots_used, 1)
                        else:
                            mm.then_inc(gu_ps, 1)
                    pe.wait_ge(y_ready, g + 2)
                    combine(g, 0)
                    pe.wait_ge(swiglu, 6 * g + 6)
                    for f in range(KC):
                        if f % 2 == 0:
                            pe.wait_ge(down_in[f // 2], 16 * e + 16)
                        for j in range(KC):
                            mm = pe.matmul(psum[:, MISC, j * SLOTS:(j + 1) * SLOTS],
                                           down_slot[f][:, j * P:(j + 1) * P], hid_sb[:, f, :],
                                           start=(f == 0 and j == 0), stop=(f == KC - 1), skip_group_check=True)
                        if f % 2 == 1 and f < KC - 1:
                            mm.then_inc(slots_used, 1)
                        if f == KC // 2 - 1:
                            combine(g, 1)
                    mm.then_inc(yT_ps, 1)
            total = pe.value_load(first_block[0:1, E:E + 1], min_val=1, max_val=4 * E)
            turn_y(total)
            for t in range(TT):
                combine(total, t)

        @block.scalar
        def _(act):
            act.wait_ge(consts_in, 48)
            act.activation(csig[:], c_sb[:], ACT.Sigmoid).then_inc(csig_ready, 1)
            for t in range(TA):
                if t == 0:
                    act.wait_ge(x_in, 16)
                if t == TT:
                    act.wait_ge(ctx_in, 16)
                src = x_sb[:, t, :] if t < TT else ctx_sb[:, t - TT, :]
                if t > 0:
                    act.wait_ge(squares, t)
                act.activation(square, src, ACT.Square, accum_out=ss[:, t:t + 1]).then_inc(squares, 1)

            def deviation(n, lo, hi):
                act.wait_ge(vars_ready, n)
                act.activation(std[:, lo:hi], var[:, lo:hi], ACT.Sqrt).then_inc(std_ready, 1)

            deviation(1, 0, TA)
            act.wait_ge(a1_ready, 2)
            for k in range(1, KC, 2):
                act.wait_ge(xT_ps, k + 1)
                for v in range(2):
                    half = slice(v * SEQ, (v + 1) * SEQ)
                    ins = act.activation(hT[:, k, half], psum[:, k % 4, half], ACT.Identity,
                                         bias=ada[:, k, v:v + 1], scale=a1[:, k, v:v + 1])
                ins.then_inc(hT_act, 1)
            for n in range(24):
                part, i = n // 8, n % 8
                act.wait_ge(proj_ps, n + 1)
                if part == 0:
                    ins = act.activation(qT[:, i, :], psum[:, n % 4, 0:SEQ], ACT.Copy, scale=HD ** -0.5)
                elif part == 1:
                    ins = act.copy(kT[:, i, :], psum[:, n % 4, :])
                else:
                    ins = act.copy(v_sb[:, i % 4, (i // 4) * BANK:(i // 4 + 1) * BANK], psum[:, n % 4, :])
                ins.then_inc(proj_sb, 1)
            for h in range(HEADS):
                act.wait_ge(negmax_ready, h + 1)
                if h < 2:
                    act.wait_ge(rows_ready, 4)
                else:
                    act.wait_ge(probsT_ps, h - 1)
                for t in range(TT):
                    act.activation(probs[h % 2][:, t, :], psum[:, 2 * (h % 2) + t, :], ACT.Exp,
                                   bias=negmax[:, h, t:t + 1],
                                   accum_out=psumexp[:, h, t:t + 1]).then_inc(probs_ready, 1)
            for j in range(1, KC, 2):
                act.wait_ge(oT_ps, j + 1)
                act.copy(oT[:, j, :], psum[:, j % 4, 0:SEQ]).then_inc(oT_act, 1)
            for t in range(TT):
                act.wait_ge(attn_out_ps, t + 1)
                act.wait_ge(squares, TA + t)
                act.activation(square, psum[:, 4 + 2 * t:6 + 2 * t, :].rearrange("p b n -> p (b n)"), ACT.Square,
                               accum_out=ss[:, 4 + t:5 + t]).then_inc(squares, 1)
            deviation(2, 4, 6)
            for t in range(TT):
                act.wait_ge(x1_ready, t + 1)
                act.wait_ge(squares, TA + 2 + t)
                act.activation(square, x_sb[:, t, :], ACT.Square, accum_out=ss[:, 6 + t:7 + t]).then_inc(squares, 1)
            deviation(3, 6, 8)
            for k in range(1, KC, 2):
                act.wait_ge(h2T_ps, k + 1)
                act.copy(h2T[:, k, :], psum[:, k % 4, 0:SEQ]).then_inc(h2T_act, 1)
            act.wait_ge(route, 1)
            for t in range(TT):
                act.activation(e4[:, t, :], top8[:, t, 0:TOPK], ACT.Exp, bias=ntop[:, t:t + 1],
                               accum_out=e4s[:, t:t + 1]).then_inc(top_exp, 1)

            def take_y(g):
                act.wait_ge(y_ps, g + 1)
                act.wait_ge(selT_sb, 2 * g + 2)
                act.activation(y_sb, psum[:, YB, :], ACT.Copy,
                               scale=gate_slot).then_inc(y_ready, 1)

            act.wait_ge(blocks_ready, 1)
            with act.Fori(0, E) as e:
                g_first = act.value_load(first_block[0:1, bass.ds(e, 1)], min_val=0, max_val=4 * E)
                g_end = act.value_load(first_block[0:1, bass.ds(e + 1, 1)], min_val=1, max_val=4 * E)
                with act.Fori(g_first, g_end) as g:
                    act.wait_ge(xg_ps, g + 1)
                    act.copy(xgT, psum[:, MISC, :].rearrange("p (k s) -> p k s", k=KC)).then_inc(xg_sb, 1)
                    take_y(g)
                    act.wait_ge(swiglu, 6 * g + 2)
                    act.activation(sig_sb, gate_sb, ACT.Sigmoid, scale=ALPHA).then_inc(sig_ready, 1)
                    act.wait_ge(yT_ps, g + 1)
                    act.copy(yT_sb, psum[:, MISC, :].rearrange("p (k s) -> p k s", k=KC)).then_inc(yT_ready, 1)
            total = act.value_load(first_block[0:1, E:E + 1], min_val=1, max_val=4 * E)
            take_y(total)
            for t in range(TT):
                act.wait_ge(fin_step, t + 1)
                act.wait_ge(squares, TA + 4 + t)
                act.activation(square, acc[:, t, :], ACT.Square, accum_out=ss[:, 8 + t:9 + t]).then_inc(squares, 1)
            deviation(4, 8, 10)

        @block.vector
        def _(dve):
            def inverse_deviation(n, n_squares, lo, hi):
                dve.wait_ge(squares, n_squares)
                dve.tensor_scalar(var[:, lo:hi], ss[:, lo:hi], 1.0 / D, EPS, ALU.mult, ALU.add).then_inc(vars_ready, 1)
                dve.wait_ge(std_ready, n)
                dve.reciprocal(rstd[:, lo:hi], std[:, lo:hi]).then_inc(rstd_ready, 1)
                dve.wait_ge(rstd_ready, n)

            dve.wait_ge(csig_ready, 1)
            dve.tensor_tensor(silu[:], c_sb[:], csig[:], ALU.mult).then_inc(silu_ready, 1)
            inverse_deviation(1, TA, 0, TA)
            for t in range(TA):
                src = x_sb[:, t, :] if t < TT else ctx_sb[:, t - TT, :]
                dve.tensor_scalar(xn[:, t, :], src, rstd[:, t:t + 1], None, ALU.mult).then_inc(xn_ready, 1)
            dve.wait_ge(ada_used, KC)
            dve.tensor_tensor(ada[:], psum[:, 4, 0:4 * KC].rearrange("p (m v) -> p m v", v=2),
                              bac[:].unsqueeze(2).to_broadcast([P, 2 * KC, 2]), ALU.add).then_inc(a1_ready, 1)
            dve.wait_ge(a1_ready, 1)
            dve.scalar_tensor_tensor(out=a1[:], in0=ada[:, KC:2 * KC, :], scalar=1.0,
                                     in1=ng0[:].unsqueeze(2).to_broadcast([P, KC, 2]),
                                     op0=ALU.add, op1=ALU.mult).then_inc(a1_ready, 1)
            dve.wait_ge(a1_ready, 2)
            for k in range(0, KC, 2):
                dve.wait_ge(xT_ps, k + 1)
                for v in range(2):
                    half = slice(v * SEQ, (v + 1) * SEQ)
                    ins = dve.tensor_scalar(hT[:, k, half], psum[:, k % 4, half], a1[:, k, v:v + 1],
                                            ada[:, k, v:v + 1], ALU.mult, ALU.add)
                ins.then_inc(hT_dve, 1)
            step = 0
            for cb in range(4):
                for k in range(KC):
                    i = cb * KC + k
                    dve.wait_ge(ring_in[i % RING], 16 * (i // RING + 1))
                    if k == 0:
                        if cb >= 1:
                            dve.wait_ge(ada_sum_ps, cb)
                        ins = dve.tensor_scalar(ada_acc, ring[i % RING], silu[:, k, 0:1], None, ALU.mult)
                    else:
                        dve.wait_ge(ada_step, step)
                        ins = dve.scalar_tensor_tensor(out=ada_acc, in0=ring[i % RING], scalar=silu[:, k, 0:1],
                                                       in1=ada_acc, op0=ALU.mult, op1=ALU.add)
                    ins.then_inc(ada_step, 1)
                    step += 1
                if cb == 0:
                    dve.wait_ge(bada_in, 64)
                dve.wait_ge(ada_step, step)
                one = ada_acc[32 * cb:32 * cb + 1, :]
                dve.tensor_tensor(one, one, bada_rows[32 * cb:32 * cb + 1, :], ALU.add).then_inc(ada_step, 1)
                step += 1
                dve.wait_ge(ada_sum_ps, cb + 1)
                total = psum[:, 6:8, :].rearrange("p b n -> p (b n)")
                if cb == 0:
                    dve.wait_ge(rows_in, 48)
                    ins = dve.tensor_tensor(g1_row, total, g1_row, ALU.mult)
                elif cb == 1:
                    ins = dve.tensor_copy(sh2_row, total)
                elif cb == 2:
                    ins = dve.scalar_tensor_tensor(out=a2_row, in0=total, scalar=1.0, in1=a2_row,
                                                   op0=ALU.add, op1=ALU.mult)
                else:
                    ins = dve.tensor_tensor(g2_row[:], total, g2_row[:], ALU.mult)
                ins.then_inc(rows_ready, 1)

            for i in range(HEADS + 2):
                if i < HEADS:
                    h = i
                    dve.wait_ge(scores_ps, h + 1)
                    dve.tensor_reduce(negmax[:, h, :], psum[:, 2 * (h % 2):2 * (h % 2) + 2, :], AX.X, ALU.max,
                                      negate=True).then_inc(negmax_ready, 1)
                if 1 <= i <= HEADS:
                    h = i - 1
                    dve.wait_ge(probsT_ps, h + 1)
                    if h >= 1:
                        dve.wait_ge(pv_ps, h)
                    dve.tensor_copy(probsT.rearrange("p k n -> p (k n)"),
                                    psum[:, 4:6, :].rearrange("p b n -> p (b n)")).then_inc(probsT_sb, 1)
                if i >= 2:
                    h = i - 2
                    dve.reciprocal(rsum[:, h, :], psumexp[:, h, :]).then_inc(rsum_ready, 1)
                    dve.wait_ge(rsum_ready, h + 1)
                    dve.wait_ge(pv_ps, h + 1)
                    dve.tensor_tensor(o_sb[:, :, h * HD:(h + 1) * HD],
                                      psum[:, 6 + h % 2, 0:TT * HD].rearrange("p (t d) -> p t d", t=TT),
                                      rsum[:, h, :].unsqueeze(2).to_broadcast([P, TT, HD]),
                                      ALU.mult).then_inc(o_ready, 1)
            for j in range(0, KC, 2):
                dve.wait_ge(oT_ps, j + 1)
                dve.tensor_copy(oT[:, j, :], psum[:, j % 4, 0:SEQ]).then_inc(oT_dve, 1)
            inverse_deviation(2, TA + 2, 4, 6)
            for t in range(TT):
                dve.scalar_tensor_tensor(out=scaled[:, t, :], in0=psum[:, 4 + 2 * t:6 + 2 * t, :].rearrange("p b n -> p (b n)"),
                                         scalar=rstd[:, 4 + t:5 + t], in1=g1_row, op0=ALU.mult,
                                         op1=ALU.mult).then_inc(res_step, 1)
                dve.wait_ge(res_step, t + 1)
                dve.tensor_tensor(x_sb[:, t, :], scaled[:, t, :], x_sb[:, t, :], ALU.add).then_inc(x1_ready, 1)
            inverse_deviation(3, TA + 4, 6, 8)
            for t in range(TT):
                dve.wait_ge(x1_ready, t + 1)
                dve.scalar_tensor_tensor(out=scaled[:, t, :], in0=x_sb[:, t, :], scalar=rstd[:, 6 + t:7 + t],
                                         in1=a2_row, op0=ALU.mult, op1=ALU.mult).then_inc(res_step, 1)
                dve.wait_ge(res_step, TT + t + 1)
                dve.tensor_tensor(h2[:, t, :], scaled[:, t, :], sh2_row, ALU.add).then_inc(h2_ready, 1)
            for k in range(0, KC, 2):
                dve.wait_ge(h2T_ps, k + 1)
                dve.tensor_copy(h2T[:, k, :], psum[:, k % 4, 0:SEQ]).then_inc(h2T_dve, 1)

            steps = [1]

            def routed(ins):
                steps[0] += 1
                ins.then_inc(route_step, 1)
                dve.wait_ge(route_step, steps[0] - 1)

            dve.wait_ge(logits_ps, 1)
            dve.wait_ge(tables_in, 48)
            routed(dve.tensor_tensor(logits[:], psum[:, 4, 0:TT * E].rearrange("p (t e) -> p t e", t=TT),
                                     br_sb[:].unsqueeze(1).to_broadcast([P, TT, E]), ALU.add))
            for t in range(TT):
                routed(dve.max(top8[:, t, :], logits[:, t, :]))
                routed(dve.max_index(idx8[:, t, :], top8[:, t, :], logits[:, t, :]))
            dve.tensor_scalar(ntop[:], top8[:, :, 0], -1.0, None, ALU.mult).then_inc(route, 1)
            routed(dve.tensor_copy(idxf[:], idx8[:]))
            for t in range(TT):
                routed(dve.tensor_tensor(eq[:, t], slot_no[:, 0:E].unsqueeze(1).to_broadcast([P, TOPK, E]),
                                         idxf[:, t, 0:TOPK].unsqueeze(2).to_broadcast([P, TOPK, E]), ALU.is_equal))
                dve.tensor_reduce(member[:, t, :], eq[:, t].rearrange("p k e -> p e k"), AX.X,
                                  ALU.add).then_inc(member_ready, 1)
            dve.wait_ge(top_exp, TT)
            routed(dve.reciprocal(e4r[:], e4s[:]))
            routed(dve.tensor_tensor(g4[:], e4[:], e4r[:].unsqueeze(2).to_broadcast([P, TT, TOPK]), ALU.mult))
            for t in range(TT):
                routed(dve.tensor_tensor(geq[:, t], eq[:, t], g4[:, t, :].unsqueeze(2).to_broadcast([P, TOPK, E]),
                                         ALU.mult))
                dve.tensor_reduce(gates[:, t, :], geq[:, t].rearrange("p k e -> p e k"), AX.X,
                                  ALU.add).then_inc(gates_ready, 1)
            dve.wait_ge(pos_ps, 1)
            dve.wait_ge(member_ready, TT)
            routed(dve.scalar_tensor_tensor(out=pos[:], in0=psum[:, 5, 0:TT * E].rearrange("p (t e) -> p t e", t=TT),
                                            scalar=1.0, in1=member[:], op0=ALU.add, op1=ALU.mult))
            routed(dve.tensor_scalar(pos[:], pos[:], -1.0, None, ALU.add))
            counts = psum[0:1, 5, 2 * E:3 * E]
            routed(dve.tensor_scalar(nblk[:], counts, float(SLOTS), 1.0, ALU.is_gt, ALU.add))
            for more in range(2, SEQ // SLOTS):
                routed(dve.scalar_tensor_tensor(out=nblk[:], in0=counts, scalar=float(more * SLOTS), in1=nblk[:],
                                                op0=ALU.is_gt, op1=ALU.add))
            routed(dve.memset(one_row[:], 1.0))
            routed(dve.memset(cum[:, 0:1], 0.0))
            routed(dve.tensor_tensor_scan(cum[:, 1:E + 1], one_row[:], nblk[:], 0.0, ALU.mult, ALU.add))
            routed(dve.tensor_copy(first_block[:], cum[:]))
            dve.wait_ge(gatesT_ps, 1)
            dve.tensor_copy(gatesT[:], psum[0:E, 6, 0:SEQ]).then_inc(gatesT_sb, 1)
            dve.memset(yT_sb, 0.0).then_inc(yT_ready, 1)
            dve.memset(y_sb, 0.0).then_inc(y_ready, 1)
            dve.memset(selT, 0.0).then_inc(selT_sb, 1)
            dve.memset(gate_slot, 0.0).then_inc(selT_sb, 1)
            dve.memset(one_row[:], 1.0).then_inc(slots_used, COUNTED)
            dve.wait_ge(bdown_ps, 1)
            for t in range(TT):
                for h in range(2):
                    dve.tensor_copy(acc[:, t, h * BANK:(h + 1) * BANK], psum[:, 2 * t + h, :]).then_inc(comb_taken, 1)
            dve.wait_ge(comb_taken, 4)
            dve.wait_ge(selT_sb, 2)
            dve.wait_ge(y_ready, 1)
            dve.wait_ge(yT_ready, 1)
            dve.wait_ge(route_step, steps[0] - 1)
            dve.memset(one_row[:], 1.0).then_inc(blocks_ready, 1)

            def add_rows(g):
                for n in range(4):
                    t, h = n // 2, n % 2
                    a = acc[:, t, :].rearrange("p (j c n) -> p j c n", c=2, n=P)[:, :, h, :]
                    dve.wait_ge(comb_ps, 4 * g + n + 1)
                    dve.wait_ge(comb_taken, 4 * g + n + 1)
                    dve.tensor_tensor(a, psum[:, COMB + h, :].rearrange("p (j n) -> p j n", n=P), a,
                                      ALU.add).then_inc(comb_taken, 1)

            with dve.Fori(0, E) as e:
                g_first = dve.value_load(first_block[0:1, bass.ds(e, 1)], min_val=0, max_val=4 * E)
                g_end = dve.value_load(first_block[0:1, bass.ds(e + 1, 1)], min_val=1, max_val=4 * E)
                with dve.Fori(g_first, g_end) as g:
                    j0 = nc.s_assert_within((g - g_first) * SLOTS, 0, SEQ - SLOTS,
                                            skip_runtime_bounds_check_because="an expert has at most SEQ / SLOTS blocks")
                    for t in range(TT):
                        ins = dve.tensor_scalar(sel[:, t], slot_no[:, bass.ds(j0, SLOTS)].unsqueeze(1)
                                                .to_broadcast([P, 2, SLOTS]),
                                                pos[:, t, bass.ds(e, 1)], None, ALU.is_equal)
                    ins.then_inc(sel_ready, 1)
                    dve.wait_ge(gu_ps, 2 * g + 1)
                    dve.tensor_tensor(gate_sb, psum[:, GATE, :].rearrange("p (k s) -> p k s", k=UC),
                                      bgu[:, bass.ds(e, 1), 0:UC].rearrange("p o k -> p (o k)").unsqueeze(2)
                                      .to_broadcast([P, UC, SLOTS]), ALU.add).then_inc(swiglu, 1)
                    dve.wait_ge(swiglu, 6 * g + 1)
                    dve.tensor_scalar(gate_sb, gate_sb, LIMIT, None, ALU.min).then_inc(swiglu, 1)
                    dve.wait_ge(gu_ps, 2 * g + 2)
                    dve.tensor_tensor(up_sb, psum[:, UP, :].rearrange("p (k s) -> p k s", k=UC),
                                      bgu[:, bass.ds(e, 1), UC:2 * UC].rearrange("p o k -> p (o k)").unsqueeze(2)
                                      .to_broadcast([P, UC, SLOTS]), ALU.add).then_inc(swiglu, 1)
                    dve.wait_ge(swiglu, 6 * g + 3)
                    dve.tensor_scalar(up_sb, up_sb, LIMIT, -LIMIT, ALU.min, ALU.max).then_inc(swiglu, 1)
                    dve.wait_ge(sig_ready, g + 1)
                    dve.tensor_tensor(sig_sb, gate_sb, sig_sb, ALU.mult).then_inc(swiglu, 1)
                    dve.wait_ge(swiglu, 6 * g + 5)
                    dve.scalar_tensor_tensor(out=hid_sb, in0=up_sb, scalar=1.0, in1=sig_sb,
                                             op0=ALU.add, op1=ALU.mult).then_inc(swiglu, 1)
                    add_rows(g)
                    dve.wait_ge(selT_ps, g + 1)
                    dve.wait_ge(y_ready, g + 2)
                    dve.tensor_copy(selT, psum[:, SELB, 0:SEQ]).then_inc(selT_sb, 1)
                    dve.tensor_copy(gate_slot, psum[:, SELB, SEQ:SEQ + 1]).then_inc(selT_sb, 1)
            total = dve.value_load(first_block[0:1, E:E + 1], min_val=1, max_val=4 * E)
            add_rows(total)
            for t in range(TT):
                dve.wait_ge(comb_taken, 4 * total + 8)
                dve.memset(ntop[:, t:t + 1], 0.0).then_inc(fin_step, 1)
            inverse_deviation(4, TA + 6, 8, 10)
            for t in range(TT):
                dve.scalar_tensor_tensor(out=acc[:, t, :], in0=acc[:, t, :], scalar=rstd[:, 8 + t:9 + t],
                                         in1=g2_row[:], op0=ALU.mult, op1=ALU.mult).then_inc(fin_step, 1)
                dve.wait_ge(fin_step, TT + t + 1)
                dve.tensor_tensor(h2[:, t, :], acc[:, t, :], x_sb[:, t, :], ALU.add).then_inc(fin_ready, 1)


def kernel(**inputs):
    import numpy as np
    import concourse.bacc as bacc
    from concourse.bass_utils import run_bass_kernel_spmd as run

    a = {n: np.asarray(v) for n, v in inputs.items()}

    def cols(v):
        return np.ascontiguousarray(np.moveaxis(v.reshape(v.shape[:-1] + (-1, P)), -1, 0))

    host = {
        "x": a["x"],
        "c_cols": np.ascontiguousarray(np.stack([cols(a["c"][0]), cols(a["c_ctx"])], axis=-1)),
        "ctx": a["ctx"],
        "w_ada": a["w_ada"],
        "b_ada_cols": cols(a["b_ada"][0, 0:2 * D]),
        "b_ada": a["b_ada"],
        "norm_cols": cols(a["norm_g"][0, 0]),
        "norm_g": a["norm_g"],
        "w_qkv": a["w_qkv"],
        "w_o": a["w_o"],
        "rpb": a["rpb"],
        "w_router": a["w_router"],
        "b_router": a["b_router"],
        "w_gu": a["w_gu"][0],
        "b_gu_cols": cols(a["b_gu"][0]),
        "w_down": a["w_down"][0],
        "b_down": a["b_down"],
    }
    nc = bacc.Bacc("TRN2", target_bir_lowering=False, num_devices=1)
    arrays, args = {}, []
    for name, v in host.items():
        arrays[f"in_{name}"] = np.ascontiguousarray(v)
        args.append(nc.dram_tensor(f"in_{name}", v.shape, F32, kind="ExternalInput").ap())
    out = nc.dram_tensor("out_0", (1, SEQ, D), F32, kind="ExternalOutput").ap()
    build(nc, *args, out)
    r = run(nc, [arrays], core_ids=[0])
    return r.results[0]["out_0"]
```

```python
from contextlib import ExitStack

import concourse.bass as bass
from concourse import mybir

F32 = mybir.dt.float32
BF16 = mybir.dt.bfloat16
I32 = mybir.dt.int32
U32 = mybir.dt.uint32
ALU = mybir.AluOpType
ACT = mybir.ActivationFunctionType
AX = mybir.AxisListType

P = 128
D = 1024
KC = D // P
SEQ = 256
CTX = 256
TT = SEQ // P
TA = (SEQ + CTX) // P
KEYS = SEQ + CTX
HEADS = 16
HD = D // HEADS
GRID_W = 64
WIN_ROWS, WIN_COLS = 8, 16
RPB_R, RPB_C = 2 * WIN_ROWS - 1, 2 * WIN_COLS - 1
ROWS = SEQ // GRID_W
BROWS = ROWS + 2
E = 32
TOPK = 4
EPS = 1e-6
LIMIT = 7.0
ALPHA = 1.702
MASKED = -1e30
SLOTS = 64
BANK = 512
GU = 2 * D
UC = D // P
RING = 4


def build(nc, x, c_cols, ctx, w_ada, b_ada_cols, b_ada, norm_cols, norm_g, w_qkv, w_o, rpb,
          w_router, b_router, w_gu, b_gu, w_down, b_down, out):
    with ExitStack() as stack:
        def sb(name, shape, dt=F32):
            return stack.enter_context(nc.sbuf_tensor(name, shape, dt))

        def sem(name):
            return stack.enter_context(nc.semaphore(name))

        psum = stack.enter_context(nc.psum_tensor("psum", [P, 8, BANK], F32))

        warena = sb("warena", [P, 3 * KC * D])
        gu_slot = [warena[:, k * GU:(k + 1) * GU] for k in range(KC)]
        dn0 = KC * GU
        down_slot = [warena[:, dn0 + f * D:dn0 + (f + 1) * D] for f in range(KC)]
        ada_slot = gu_slot
        q_words = KC * BANK
        qkv_at = [dn0, dn0 + q_words] + [b * q_words for b in range(4)]
        qkv_blk = [warena[:, a:a + q_words].rearrange("p (k n) -> p k n", k=KC) for a in qkv_at]
        bias0 = 3 * KC * D - HEADS * BROWS * GRID_W
        bias = warena[:, bias0:].rearrange("p (h r w) -> p h r w", h=HEADS, r=BROWS)
        bada_rows = warena[:, bias0 - D:bias0]
        wo_sb = warena[:, 0:KC * D].rearrange("p (k n) -> p k n", k=KC)

        parena = sb("parena", [P, 14 * D])
        hT = parena[:, 0:4 * D].rearrange("p (k n) -> p k n", k=KC)
        xn = parena[:, 4 * D:8 * D].rearrange("p (t n) -> p t n", t=TA)
        kT = parena[:, 4 * D:8 * D].rearrange("p (k n) -> p k n", k=KC)
        v_sb = parena[:, 8 * D:12 * D].rearrange("p (t n) -> p t n", t=TA)
        qT = parena[:, 12 * D:14 * D].rearrange("p (k n) -> p k n", k=KC)
        oT = parena[:, 2 * D:4 * D].rearrange("p (k n) -> p k n", k=KC)
        acc = parena[:, 4 * D:6 * D].rearrange("p (t n) -> p t n", t=TT)
        h2T = parena[:, 6 * D:8 * D].rearrange("p (k n) -> p k n", k=KC)
        square = parena[:, 8 * D:9 * D]
        scaled = parena[:, 9 * D:11 * D].rearrange("p (t n) -> p t n", t=TT)

        bd_sb = parena[0:E, 11 * D:12 * D]
        eq, geq = (parena[:, 12 * D + i * 256:12 * D + (i + 1) * 256]
                   .rearrange("p (t k e) -> p t k e", t=TT, k=TOPK) for i in range(2))

        x_sb = sb("x_sb", [P, TT, D])
        h2 = sb("h2", [P, TT, D])
        ctx_sb = h2
        ring2 = h2[:].rearrange("p t n -> p (t n)")
        g2_row = sb("g2_row", [P, D])

        work = sb("work", [P, 6 * D])
        g1_row, sh2_row, a2_row = (work[:, i * D:(i + 1) * D] for i in range(3))
        ada_acc = work[:, 3 * D:4 * D]
        ada_rows = work[:, 3 * D:3 * D + BANK]
        ring = [ring2[:, 0:D], ring2[:, D:2 * D], work[:, 4 * D:5 * D], work[:, 5 * D:6 * D]]
        probs = [work[:, (3 + i) * D:(4 + i) * D].rearrange("p (t n) -> p t n", t=TT) for i in range(2)]
        probsT = [a.rearrange("p (k n) -> p k n", k=TA) for a in (work[:, 5 * D:6 * D], parena[:, 0:D])]
        xg_sb, gate_sb, up_sb, sig_sb, hid_sb, y_sb = (work[:, i * BANK:(i + 1) * BANK] for i in range(6))
        xgT, hidT = (work[:, i * BANK:(i + 1) * BANK].rearrange("p (c h s) -> p c h s", c=KC // 2, h=2)
                     for i in (6, 7))
        sel = work[:, 8 * BANK:8 * BANK + TT * SLOTS].rearrange("p (t s) -> p t s", t=TT)
        sel_gate = work[:, 9 * BANK:9 * BANK + TT * 2 * SLOTS].rearrange("p (t c s) -> p t c s", t=TT, c=2)
        selT = work[:, 10 * BANK:10 * BANK + SEQ]
        bgu_raw = ring2[0:3 * E, :]
        bgu3 = sb("bgu3", [3 * E, GU], BF16)
        expert_no = sb("expert_no", [3 * E, 1])
        pick = sb("pick", [3 * E, SLOTS], BF16)

        wr_sb = sb("wr_sb", [P, KC, E])
        br_sb = sb("br_sb", [P, E])
        ident = sb("ident", [P, P])
        flip = sb("flip", [P, P])
        before = sb("before", [P, P])
        ones = sb("ones", [P, P])
        slot_no = sb("slot_no", [P, SEQ])
        c_sb = sb("c_sb", [P, KC, 2])
        csig = sb("csig", [P, KC, 2])
        silu = sb("silu", [P, KC, 32])
        bac = sb("bac", [P, 2 * KC])
        ng0 = sb("ng0", [P, KC])
        ada = sb("ada", [P, 2 * KC, 2])
        a1 = sb("a1", [P, KC, 2])
        ss = sb("ss", [P, 12])
        var = sb("var", [P, 12])
        std = sb("std", [P, 12])
        rstd = sb("rstd", [P, 12])
        negmax = sb("negmax", [P, HEADS, TT])
        psumexp = sb("psumexp", [P, HEADS, TT])
        rsum = sb("rsum", [P, HEADS, TT])
        logits = parena[:, 13 * D + SEQ:13 * D + SEQ + TT * E].rearrange("p (t e) -> p t e", t=TT)
        top8 = sb("top8", [P, TT, 8])
        idx8 = sb("idx8", [P, TT, 8], U32)
        idxf = sb("idxf", [P, TT, 8])
        ntop = sb("ntop", [P, TT])
        e4 = sb("e4", [P, TT, TOPK])
        e4s = sb("e4s", [P, TT])
        e4r = sb("e4r", [P, TT])
        g4 = sb("g4", [P, TT, TOPK])
        member = parena[:, 13 * D + 2 * SEQ:13 * D + 2 * SEQ + TT * E].rearrange("p (t e) -> p t e", t=TT)
        gates = sb("gates", [P, TT, E])
        gatesT = parena[0:E, 13 * D:13 * D + SEQ]
        pos = sb("pos", [P, TT, E])
        nblk = sb("nblk", [1, E])
        one_row = sb("one_row", [1, E])
        cum = sb("cum", [1, E + 1])
        first_block = sb("first_block", [1, E + 1], I32)

        x_in, ctx_in, consts_in, tables_in, rows_in, bias_in, wo_in, out_done = (
            sem(n) for n in ("x_in", "ctx_in", "consts_in", "tables_in", "rows_in", "bias_in", "wo_in", "out_done"))
        ada_in = [sem(f"ada_in{k}") for k in range(KC)]
        qkv_in = [sem(f"qkv_in{b}") for b in range(6)]
        ring_in = [sem(f"ring_in{r}") for r in range(RING)]
        bada_in, bdown_in = sem("bada_in"), sem("bdown_in")
        const_ready, bias_masked = sem("const_ready"), sem("bias_masked")
        csig_ready, silu_ready = sem("csig_ready"), sem("silu_ready")
        squares, vars_ready, std_ready, rstd_ready, xn_ready = (
            sem(n) for n in ("squares", "vars_ready", "std_ready", "rstd_ready", "xn_ready"))
        ada_used, ada_ready, a1_ready = sem("ada_used"), sem("ada_ready"), sem("a1_ready")
        xT_ps, hT_dve, hT_act = sem("xT_ps"), sem("hT_dve"), sem("hT_act")
        proj_ps, proj_sb = sem("proj_ps"), sem("proj_sb")
        ada_step, ada_sum_ps, rows_ready = sem("ada_step"), sem("ada_sum_ps"), sem("rows_ready")
        scores_ps, negmax_ready, probs_ready = sem("scores_ps"), sem("negmax_ready"), sem("probs_ready")
        probsT_ps, probsT_sb, pv_ps, rsum_ready = (
            sem(n) for n in ("probsT_ps", "probsT_sb", "pv_ps", "rsum_ready"))
        oT_ready, attn_out_ps, norm_ready = sem("oT_ready"), sem("attn_out_ps"), sem("norm_ready")
        bgu_in, bgu_step, adaT_ps, ada_rows_ps, ada_rows_sb = (
            sem(n) for n in ("bgu_in", "bgu_step", "adaT_ps", "ada_rows_ps", "ada_rows_sb"))
        res_step, x1_ready, h2_ready = sem("res_step"), sem("x1_ready"), sem("h2_ready")
        h2T_ps, h2T_dve, h2T_act, logits_ps = sem("h2T_ps"), sem("h2T_dve"), sem("h2T_act"), sem("logits_ps")
        route_step = sem("route_step")
        route, top_exp, member_ready, gates_ready, pos_ps = (
            sem(n) for n in ("route", "top_exp", "member_ready", "gates_ready", "pos_ps"))
        gatesT_ps, gatesT_sb, bdown_ps, blocks_ready = (
            sem(n) for n in ("gatesT_ps", "gatesT_sb", "bdown_ps", "blocks_ready"))
        gu_in = [sem(f"gu_in{k}") for k in range(KC)]
        down_in = [sem(f"down_in{k}") for k in range(KC // 2)]
        slots_used, sel_ready, selT_ps, selT_sb = (
            sem(n) for n in ("slots_used", "sel_ready", "selT_ps", "selT_sb"))
        xg_ps, xg_sb_ready, gu_ps, swiglu, sig_ready = (
            sem(n) for n in ("xg_ps", "xg_sb_ready", "gu_ps", "swiglu", "sig_ready"))
        xgT_ps, xgT_sb, hidT_ps, hidT_sb = (sem(n) for n in ("xgT_ps", "xgT_sb", "hidT_ps", "hidT_sb"))
        y_ps, y_ready, comb_ps, comb_taken = (
            sem(n) for n in ("y_ps", "y_ready", "comb_ps", "comb_taken"))
        fin_step, fin_ready = sem("fin_step"), sem("fin_ready")

        block = stack.enter_context(nc.Block())
        N_CONST = 12
        USES = KC + KC // 2
        COUNTED = USES - 2
        XG, TURN, GATE, UP, YB, COMB, SELB = 0, 1, 2, 3, 4, 5, 7

        def expert_slot_dma(sp, s, e):
            if s < KC:
                src = w_gu[bass.ds(e, 1), s * P:(s + 1) * P, :].rearrange("o p n -> (o p) n")
                sp.dma_start(gu_slot[s], src).then_inc(gu_in[s], 16)
            else:
                f = s - KC
                src = w_down[bass.ds(e, 1), 2 * f * P:2 * (f + 1) * P, :].rearrange("o (c p) n -> (o p) c n", c=2)
                dst = warena[:, dn0 + 2 * f * D:dn0 + 2 * (f + 1) * D].rearrange("p (c n) -> p c n", c=2)
                sp.dma_start(dst, src).then_inc(down_in[f], 16)

        @block.sync
        def _(sp):
            sp.dma_start(c_sb[:], c_cols).then_inc(consts_in, 16)
            sp.dma_start(bac[:], b_ada_cols).then_inc(consts_in, 16)
            sp.dma_start(ng0[:], norm_cols).then_inc(consts_in, 16)
            sp.dma_start(x_sb[:], x[0].rearrange("(t p) n -> p t n", p=P)).then_inc(x_in, 16)
            sp.dma_start(ctx_sb[:], ctx[0].rearrange("(t p) n -> p t n", p=P)).then_inc(ctx_in, 16)
            for k in range(KC):
                sp.dma_start(ada_slot[k], w_ada[0, k * P:(k + 1) * P, 0:2 * D]).then_inc(ada_in[k], 16)
            wq = w_qkv[0].rearrange("(k p) n -> p k n", p=P)
            for b in range(6):
                if b >= 2:
                    sp.wait_ge(ada_used, 2 * (b - 1))
                sp.dma_start(qkv_blk[b], wq[:, :, b * BANK:(b + 1) * BANK]).then_inc(qkv_in[b], 16)
            sp.wait_ge(proj_ps, 8)
            for i in range(4):
                sp.dma_start(bada_rows[32 * i:32 * i + 1, :], b_ada[0:1, (2 + i) * D:(3 + i) * D]).then_inc(bada_in, 16)
            for a in range(2):
                for r in range(BROWS):
                    row = WIN_ROWS - 1 - 2 - a + r
                    src = bass.AP(tensor=rpb.tensor, offset=row * RPB_C + WIN_COLS - 1 - (GRID_W - 1),
                                  ap=[[1, GRID_W], [RPB_R * RPB_C, HEADS], [1, GRID_W]])
                    sp.dma_start(bias[GRID_W * a:GRID_W * (a + 1), :, r, :], src).then_inc(bias_in, 16)
            sp.dma_start(wr_sb[:], w_router[0].rearrange("(k p) e -> p k e", p=P)).then_inc(tables_in, 16)
            sp.dma_start(br_sb[:], b_router.to_broadcast([P, E])).then_inc(tables_in, 16)
            sp.wait_ge(proj_ps, 16)
            sp.dma_start(wo_sb, w_o[0].rearrange("(k p) n -> p k n", p=P)).then_inc(wo_in, 16)
            sp.wait_ge(proj_ps, 24)
            for s in range(4, KC):
                expert_slot_dma(sp, s, 0)
            sp.wait_ge(rows_ready, 4)
            for part in range(3):
                sp.dma_start(bgu_raw[part * E:(part + 1) * E, :], b_gu).then_inc(bgu_in, 16)
            sp.wait_ge(scores_ps, HEADS)
            for s in range(KC, USES):
                expert_slot_dma(sp, s, 0)
            sp.wait_ge(attn_out_ps, TT)
            sp.dma_start(bd_sb, b_down[0]).then_inc(bdown_in, 16)
            for s in range(4):
                expert_slot_dma(sp, s, 0)
            sp.wait_ge(blocks_ready, 1)
            with sp.Fori(1, E) as e:
                done = sp.value_load(first_block[0:1, bass.ds(e, 1)], min_val=1, max_val=4 * E)
                for s in range(USES):
                    if s == KC - 1:
                        sp.wait_ge(gu_ps, 2 * done)
                    elif s == USES - 1:
                        sp.wait_ge(y_ps, done)
                    else:
                        sp.wait_ge(slots_used, COUNTED * done + (s + 1 if s < KC else s))
                    expert_slot_dma(sp, s, e)
            for t in range(TT):
                sp.wait_ge(fin_ready, t + 1)
                sp.dma_start(out[0, t * P:(t + 1) * P, :], h2[:, t, :]).then_inc(out_done, 16)
            sp.wait_ge(out_done, 16 * TT)

        @block.gpsimd
        def _(pool):
            made = 0

            def make(ins):
                nonlocal made
                made += 1
                ins.then_inc(const_ready, 1)
                pool.wait_ge(const_ready, made)

            make(pool.memset(ident[:], 0.0))
            make(pool.memset(flip[:], 0.0))
            make(pool.memset(before[:], 1.0))
            make(pool.memset(ones[:], 1.0))
            make(pool.affine_select(out=ident[:], in_=ident[:], compare_op=ALU.not_equal, fill=1.0, base=0,
                                    pattern=[[-1, P]], channel_multiplier=1))
            for a in range(2):
                blk = flip[GRID_W * a:GRID_W * (a + 1), GRID_W * a:GRID_W * (a + 1)]
                make(pool.affine_select(out=blk, in_=blk, compare_op=ALU.not_equal, fill=1.0, base=-(GRID_W - 1),
                                        pattern=[[1, GRID_W]], channel_multiplier=1))
            make(pool.affine_select(out=before[:], in_=before[:], compare_op=ALU.is_gt, fill=0.0, base=0,
                                    pattern=[[1, P]], channel_multiplier=-1))
            make(pool.iota(slot_no[:], pattern=[[1, SEQ]], base=0, channel_multiplier=0,
                           allow_small_or_imprecise_dtypes=True))
            for part in range(3):
                make(pool.iota(expert_no[part * E:(part + 1) * E, :], pattern=[[0, 1]], base=0, channel_multiplier=1,
                               allow_small_or_imprecise_dtypes=True))
            for i, row in ((1, g1_row), (2, a2_row), (3, g2_row[:])):
                pool.dma_start(row, norm_g[0, i:i + 1, :].to_broadcast([P, D])).then_inc(rows_in, 16)
            for i in range(4 * KC):
                cb, k = i // KC, i % KC
                if i == 0:
                    pool.wait_ge(xn_ready, TA)
                if i >= RING:
                    last = i - RING
                    pool.wait_ge(ada_step, (KC + 1) * (last // KC) + last % KC + 1)
                pool.dma_start(ring[i % RING], w_ada[0, k * P:(k + 1) * P, (2 + cb) * D:(3 + cb) * D]) \
                    .then_inc(ring_in[i % RING], 16)
            pool.wait_ge(bias_in, 16 * 2 * BROWS)
            for a in range(2):
                tab = bias[GRID_W * a:GRID_W * (a + 1)].rearrange("p h r w -> p (h r) w")
                lo = tab[:, :, 0:GRID_W - WIN_COLS]
                hi = tab[:, :, WIN_COLS:GRID_W]
                n = GRID_W - WIN_COLS
                pool.affine_select(out=lo, in_=lo, compare_op=ALU.is_ge, fill=MASKED,
                                   base=WIN_COLS // 2 - (GRID_W - 1), pattern=[[0, HEADS * BROWS], [1, n]],
                                   channel_multiplier=1).then_inc(bias_masked, 1)
                pool.wait_ge(bias_masked, 2 * a + 1)
                pool.affine_select(out=hi, in_=hi, compare_op=ALU.is_ge, fill=MASKED,
                                   base=GRID_W - 1 + WIN_COLS // 2 - 1 - WIN_COLS,
                                   pattern=[[0, HEADS * BROWS], [-1, n]],
                                   channel_multiplier=-1).then_inc(bias_masked, 1)
                pool.wait_ge(bias_masked, 2 * a + 2)
            pool.wait_ge(bgu_in, 48)
            split = 0

            def part_of(ins):
                nonlocal split
                split += 1
                ins.then_inc(bgu_step, 1)
                pool.wait_ge(bgu_step, split)

            part_of(pool.tensor_copy(bgu3[:], bgu_raw))
            part_of(pool.tensor_tensor(bgu_raw, bgu_raw, bgu3[:], ALU.subtract))
            part_of(pool.tensor_copy(bgu3[E:2 * E, :], bgu_raw[E:2 * E, :]))
            third = slice(2 * E, 3 * E)
            part_of(pool.tensor_copy(bgu3[third, :], bgu_raw[third, :]))
            part_of(pool.tensor_tensor(bgu_raw[third, :], bgu_raw[third, :], bgu3[third, :], ALU.subtract))
            part_of(pool.tensor_copy(bgu3[third, :], bgu_raw[third, :]))

        @block.tensor
        def _(pe):
            pe.wait_ge(const_ready, N_CONST)
            pe.wait_ge(silu_ready, 2)
            for k in range(KC):
                pe.wait_ge(ada_in[k], 16)
                for b in range(4):
                    mm = pe.matmul(psum[32 * b:32 * (b + 1), 4, :], silu[:, k, :],
                                   ada_slot[k][:, b * BANK:(b + 1) * BANK], start=(k == 0), stop=(k == KC - 1))
                mm.then_inc(ada_used, 1)
            pe.wait_ge(ada_rows_sb, 1)
            for c in range(4):
                mm = pe.transpose(psum[:, 5, c * P:(c + 1) * P], ada_rows[:, c * P:(c + 1) * P], ident[:])
            mm.then_inc(adaT_ps, 1)
            pe.wait_ge(xn_ready, TA)
            for k in range(KC):
                if k >= 4:
                    pe.wait_ge(hT_dve if k % 2 == 0 else hT_act, k // 2 - 1)
                for t in range(TA):
                    mm = pe.transpose(psum[:, k % 4, t * P:(t + 1) * P], xn[:, t, k * P:(k + 1) * P], ident[:])
                mm.then_inc(xT_ps, 1)

            def ada_sum(cb):
                pe.wait_ge(ada_step, (KC + 1) * (cb + 1))
                if cb >= 1:
                    pe.wait_ge(rows_ready, cb)
                for h in range(2):
                    mm = pe.matmul(psum[:, 6 + h, :], ones[:], ada_acc[:, h * BANK:(h + 1) * BANK],
                                   start=True, stop=True)
                mm.then_inc(ada_sum_ps, 1)

            pe.wait_ge(hT_dve, KC // 2)
            pe.wait_ge(hT_act, KC // 2)
            for n in range(24):
                part, i = n // 8, n % 8
                blk = n // 4
                if n % 4 == 0:
                    pe.wait_ge(qkv_in[blk], 16)
                if n >= 4:
                    pe.wait_ge(proj_sb, n - 3)
                w = qkv_blk[blk]
                for k in range(KC):
                    if part < 2:
                        j = n % 4
                        width = SEQ if part == 0 else KEYS
                        mm = pe.matmul(psum[:, n % 4, 0:width], w[:, k, j * P:(j + 1) * P], hT[:, k, 0:width],
                                       start=(k == 0), stop=(k == KC - 1))
                    else:
                        t = n % 4
                        mm = pe.matmul(psum[:, n % 4, :], hT[:, k, t * P:(t + 1) * P], w[:, k, :],
                                       start=(k == 0), stop=(k == KC - 1))
                mm.then_inc(proj_ps, 1)
                if n in (13, 16, 19, 22):
                    ada_sum((13, 16, 19, 22).index(n))

            def scores(h):
                j, r = h // 2, HD * (h % 2)
                if h < 2:
                    pe.wait_ge(proj_sb, 24)
                    pe.wait_ge(bias_masked, 4)
                else:
                    pe.wait_ge(probs_ready, 2 * (h - 1))
                for t in range(TT):
                    s = psum[:, 2 * (h % 2) + t, :]
                    pe.matmul(s[:, 0:KEYS], qT[r:r + HD, j, t * P:(t + 1) * P], kT[r:r + HD, j, :],
                              start=True, stop=False)
                    mm = pe.matmul(s[:, 0:SEQ], flip[:],
                                   bias[:, h, 2 - 2 * t:2 - 2 * t + ROWS, :].rearrange("p r w -> p (r w)"),
                                   start=False, stop=True)
                mm.then_inc(scores_ps, 1)

            def turn_probs(h):
                pe.wait_ge(norm_ready, h + 1)
                if h >= 1:
                    pe.wait_ge(probsT_sb, h)
                for k in range(TA):
                    for t in range(TT):
                        o = (k % 2) * SEQ + t * P
                        mm = pe.transpose(psum[:, 4 + k // 2, o:o + P], probs[h % 2][:, t, k * P:(k + 1) * P], ident[:])
                mm.then_inc(probsT_ps, 1)

            def values(j):
                pe.wait_ge(probsT_sb, 2 * j + 2)
                if j < 2:
                    pe.wait_ge(rows_ready, 4)
                else:
                    pe.wait_ge(oT_ready, j - 1)
                for k in range(TA):
                    for o in range(2):
                        h = 2 * j + o
                        mm = pe.matmul(psum[o * HD:(o + 1) * HD, 6 + j % 2, 0:SEQ], v_sb[:, k, h * HD:(h + 1) * HD],
                                       probsT[o][:, k, :], start=(k == 0), stop=(k == TA - 1))
                mm.then_inc(pv_ps, 1)

            for i in range(HEADS + 2):
                if i < HEADS:
                    scores(i)
                if 1 <= i <= HEADS:
                    turn_probs(i - 1)
                if i >= 2 and i % 2 == 1:
                    values((i - 3) // 2)

            pe.wait_ge(oT_ready, KC)
            pe.wait_ge(wo_in, 16)
            for t in range(TT):
                for h in range(2):
                    for j in range(KC):
                        mm = pe.matmul(psum[:, 4 + 2 * t + h, :], oT[:, j, t * P:(t + 1) * P],
                                       wo_sb[:, j, h * BANK:(h + 1) * BANK], start=(j == 0), stop=(j == KC - 1))
                mm.then_inc(attn_out_ps, 1)

            pe.wait_ge(h2_ready, TT)
            for k in range(KC):
                if k >= 4:
                    pe.wait_ge(h2T_dve if k % 2 == 0 else h2T_act, k // 2 - 1)
                for t in range(TT):
                    mm = pe.transpose(psum[:, k % 4, t * P:(t + 1) * P], h2[:, t, k * P:(k + 1) * P], ident[:])
                mm.then_inc(h2T_ps, 1)
            pe.wait_ge(h2T_dve, KC // 2)
            pe.wait_ge(h2T_act, KC // 2)
            pe.wait_ge(tables_in, 16 * 2)
            for t in range(TT):
                for k in range(KC):
                    mm = pe.matmul(psum[:, 4, t * E:(t + 1) * E], h2T[:, k, t * P:(t + 1) * P], wr_sb[:, k, :],
                                   start=(k == 0), stop=(k == KC - 1))
            mm.then_inc(logits_ps, 1)
            pe.wait_ge(member_ready, TT)
            pe.matmul(psum[:, 5, 0:E], before[:], member[:, 0, :], start=True, stop=True)
            pe.matmul(psum[:, 5, E:2 * E], ones[:], member[:, 0, :], start=True, stop=False)
            pe.matmul(psum[:, 5, E:2 * E], before[:], member[:, 1, :], start=False, stop=True)
            pe.matmul(psum[:, 5, 2 * E:3 * E], ones[:], member[:, 0, :], start=True, stop=False)
            pe.matmul(psum[:, 5, 2 * E:3 * E], ones[:], member[:, 1, :], start=False, stop=True).then_inc(pos_ps, 1)
            pe.wait_ge(gates_ready, TT)
            for t in range(TT):
                mm = pe.transpose(psum[0:E, 6, t * P:(t + 1) * P], gates[:, t, :], ident[:])
            mm.then_inc(gatesT_ps, 1)
            pe.wait_ge(gatesT_sb, 1)
            pe.wait_ge(bdown_in, 16)
            for t in range(TT):
                for h in range(2):
                    mm = pe.matmul(psum[:, 2 * t + h, :], gatesT[:, t * P:(t + 1) * P],
                                   bd_sb[:, h * BANK:(h + 1) * BANK], start=True, stop=True)
            mm.then_inc(bdown_ps, 1)

            def combine(g, n):
                t, h = n // 2, n % 2
                if n == 0:
                    pe.wait_ge(y_ready, g + 1)
                    pe.wait_ge(selT_sb, g + 1)
                pe.wait_ge(comb_taken, 4 * g + n + 3)
                half = slice(h * SLOTS, (h + 1) * SLOTS)
                pe.matmul(psum[:, COMB + h, :], selT[half, t * P:(t + 1) * P], y_sb[half, :],
                          start=True, stop=True).then_inc(comb_ps, 1)

            pe.wait_ge(blocks_ready, 1)
            pe.wait_ge(bgu_step, 6)
            pe.wait_ge(comb_taken, 4)
            with pe.Fori(0, E) as e:
                g_first = pe.value_load(first_block[0:1, bass.ds(e, 1)], min_val=0, max_val=4 * E)
                g_end = pe.value_load(first_block[0:1, bass.ds(e + 1, 1)], min_val=1, max_val=4 * E)
                with pe.Fori(g_first, g_end) as g:
                    pe.wait_ge(sel_ready, g + 1)
                    pe.wait_ge(selT_sb, g + 1)
                    for t in range(TT):
                        mm = pe.transpose(psum[:, SELB, t * P:(t + 1) * P],
                                          sel_gate[:, t].rearrange("p c s -> p (c s)"), ident[:])
                    mm.then_inc(selT_ps, 1)
                    for t in range(TT):
                        for h in range(2):
                            mm = pe.matmul(psum[h * SLOTS:(h + 1) * SLOTS, XG, :], sel[:, t, :],
                                           h2[:, t, h * BANK:(h + 1) * BANK], start=(t == 0), stop=(t == TT - 1))
                    mm.then_inc(xg_ps, 1)
                    combine(g, 0)
                    pe.wait_ge(xg_sb_ready, g + 1)
                    for c in range(KC // 2):
                        mm = pe.transpose(psum[:, TURN, c * P:(c + 1) * P], xg_sb[:, c * P:(c + 1) * P], ident[:])
                    mm.then_inc(xgT_ps, 1)
                    combine(g, 1)
                    for b in range(2):
                        for h in range(2):
                            c0 = b * D + h * BANK
                            pe.matmul(psum[h * SLOTS:(h + 1) * SLOTS, GATE + b, :], pick[:], bgu3[:, c0:c0 + BANK],
                                      start=True, stop=False)
                    pe.wait_ge(xgT_sb, g + 1)
                    for k in range(KC):
                        pe.wait_ge(gu_in[k], 16 * e + 16)
                        for b in range(2):
                            for h in range(2):
                                c0 = b * D + h * BANK
                                mm = pe.matmul(psum[h * SLOTS:(h + 1) * SLOTS, GATE + b, :], xgT[:, k % 4, k // 4, :],
                                               gu_slot[k][:, c0:c0 + BANK], start=False, stop=(k == KC - 1))
                            if k == KC - 1:
                                mm.then_inc(gu_ps, 1)
                        if k < KC - 1:
                            mm.then_inc(slots_used, 1)
                    combine(g, 2)
                    combine(g, 3)
                    pe.wait_ge(swiglu, 4 * g + 4)
                    for c in range(KC // 2):
                        mm = pe.transpose(psum[:, TURN, c * P:(c + 1) * P], hid_sb[:, c * P:(c + 1) * P], ident[:])
                    mm.then_inc(hidT_ps, 1)
                    pe.wait_ge(hidT_sb, g + 1)
                    for f in range(KC):
                        if f % 2 == 0:
                            pe.wait_ge(down_in[f // 2], 16 * e + 16)
                        for h in range(2):
                            mm = pe.matmul(psum[h * SLOTS:(h + 1) * SLOTS, YB, :], hidT[:, f % 4, f // 4, :],
                                           down_slot[f][:, h * BANK:(h + 1) * BANK],
                                           start=(f == 0), stop=(f == KC - 1))
                        if f == KC - 1:
                            mm.then_inc(y_ps, 1)
                        elif f % 2 == 1:
                            mm.then_inc(slots_used, 1)
            total = pe.value_load(first_block[0:1, E:E + 1], min_val=1, max_val=4 * E)
            for n in range(4):
                combine(total, n)

        @block.scalar
        def _(act):
            act.wait_ge(consts_in, 48)
            act.activation(csig[:], c_sb[:], ACT.Sigmoid).then_inc(csig_ready, 1)
            for t in range(TA):
                if t == 0:
                    act.wait_ge(x_in, 16)
                if t == TT:
                    act.wait_ge(ctx_in, 16)
                src = x_sb[:, t, :] if t < TT else ctx_sb[:, t - TT, :]
                if t > 0:
                    act.wait_ge(squares, t)
                act.activation(square, src, ACT.Square, accum_out=ss[:, t:t + 1]).then_inc(squares, 1)

            def deviation(n, lo, hi):
                act.wait_ge(vars_ready, n)
                act.activation(std[:, lo:hi], var[:, lo:hi], ACT.Sqrt).then_inc(std_ready, 1)

            deviation(1, 0, TA)
            act.wait_ge(a1_ready, 2)
            for k in range(1, KC, 2):
                act.wait_ge(xT_ps, k + 1)
                for v in range(2):
                    half = slice(v * SEQ, (v + 1) * SEQ)
                    ins = act.activation(hT[:, k, half], psum[:, k % 4, half], ACT.Identity,
                                         bias=ada[:, k, v:v + 1], scale=a1[:, k, v:v + 1])
                ins.then_inc(hT_act, 1)
            for n in range(24):
                part, i = n // 8, n % 8
                act.wait_ge(proj_ps, n + 1)
                if part == 0:
                    ins = act.activation(qT[:, i, :], psum[:, n % 4, 0:SEQ], ACT.Copy, scale=HD ** -0.5)
                elif part == 1:
                    ins = act.copy(kT[:, i, :], psum[:, n % 4, :])
                else:
                    ins = act.copy(v_sb[:, i % 4, (i // 4) * BANK:(i // 4 + 1) * BANK], psum[:, n % 4, :])
                ins.then_inc(proj_sb, 1)
            def take_heads(j):
                act.wait_ge(pv_ps, j + 1)
                act.copy(oT[:, j, :], psum[:, 6 + j % 2, 0:SEQ]).then_inc(oT_ready, 1)

            for h in range(HEADS):
                act.wait_ge(negmax_ready, h + 1)
                if h < 2:
                    act.wait_ge(rows_ready, 4)
                else:
                    act.wait_ge(probsT_ps, h - 1)
                for t in range(TT):
                    act.activation(probs[h % 2][:, t, :], psum[:, 2 * (h % 2) + t, :], ACT.Exp,
                                   bias=negmax[:, h, t:t + 1],
                                   accum_out=psumexp[:, h, t:t + 1]).then_inc(probs_ready, 1)
                if h >= 3 and h % 2 == 1:
                    take_heads((h - 3) // 2)
            take_heads(KC - 1)
            for t in range(TT):
                act.wait_ge(attn_out_ps, t + 1)
                act.wait_ge(squares, TA + t)
                act.activation(square, psum[:, 4 + 2 * t:6 + 2 * t, :].rearrange("p b n -> p (b n)"), ACT.Square,
                               accum_out=ss[:, 4 + t:5 + t]).then_inc(squares, 1)
            deviation(2, 4, 6)
            for t in range(TT):
                act.wait_ge(x1_ready, t + 1)
                act.wait_ge(squares, TA + 2 + t)
                act.activation(square, x_sb[:, t, :], ACT.Square, accum_out=ss[:, 6 + t:7 + t]).then_inc(squares, 1)
            deviation(3, 6, 8)
            for k in range(1, KC, 2):
                act.wait_ge(h2T_ps, k + 1)
                act.copy(h2T[:, k, :], psum[:, k % 4, 0:SEQ]).then_inc(h2T_act, 1)
            act.wait_ge(route, 1)
            for t in range(TT):
                act.activation(e4[:, t, :], top8[:, t, 0:TOPK], ACT.Exp, bias=ntop[:, t:t + 1],
                               accum_out=e4s[:, t:t + 1]).then_inc(top_exp, 1)

            act.wait_ge(blocks_ready, 1)
            turned = psum[:, TURN, :].rearrange("p (c h s) -> p c h s", c=KC // 2, h=2)
            with act.Fori(0, E) as e:
                g_first = act.value_load(first_block[0:1, bass.ds(e, 1)], min_val=0, max_val=4 * E)
                g_end = act.value_load(first_block[0:1, bass.ds(e + 1, 1)], min_val=1, max_val=4 * E)
                with act.Fori(g_first, g_end) as g:
                    act.wait_ge(xg_ps, g + 1)
                    act.copy(xg_sb, psum[:, XG, :]).then_inc(xg_sb_ready, 1)
                    act.wait_ge(xgT_ps, g + 1)
                    act.copy(xgT, turned).then_inc(xgT_sb, 1)
                    act.wait_ge(swiglu, 4 * g + 1)
                    act.activation(sig_sb, gate_sb, ACT.Sigmoid, scale=ALPHA).then_inc(sig_ready, 1)
                    act.wait_ge(hidT_ps, g + 1)
                    act.copy(hidT, turned).then_inc(hidT_sb, 1)
                    act.wait_ge(y_ps, g + 1)
                    act.copy(y_sb, psum[:, YB, :]).then_inc(y_ready, 1)
            for t in range(TT):
                act.wait_ge(fin_step, t + 1)
                act.wait_ge(squares, TA + 4 + t)
                act.activation(square, acc[:, t, :], ACT.Square, accum_out=ss[:, 8 + t:9 + t]).then_inc(squares, 1)
            deviation(4, 8, 10)

        @block.vector
        def _(dve):
            def inverse_deviation(n, n_squares, lo, hi):
                dve.wait_ge(squares, n_squares)
                dve.tensor_scalar(var[:, lo:hi], ss[:, lo:hi], 1.0 / D, EPS, ALU.mult, ALU.add).then_inc(vars_ready, 1)
                dve.wait_ge(std_ready, n)
                dve.reciprocal(rstd[:, lo:hi], std[:, lo:hi]).then_inc(rstd_ready, 1)
                dve.wait_ge(rstd_ready, n)

            dve.memset(silu[:], 0.0).then_inc(silu_ready, 1)
            dve.wait_ge(csig_ready, 1)
            dve.wait_ge(silu_ready, 1)
            dve.tensor_tensor(silu[:, :, 0:2], c_sb[:], csig[:], ALU.mult).then_inc(silu_ready, 1)
            inverse_deviation(1, TA, 0, TA)
            for t in range(TA):
                src = x_sb[:, t, :] if t < TT else ctx_sb[:, t - TT, :]
                dve.tensor_scalar(xn[:, t, :], src, rstd[:, t:t + 1], None, ALU.mult).then_inc(xn_ready, 1)
            dve.wait_ge(ada_used, KC)
            dve.tensor_copy(ada_rows, psum[:, 4, :]).then_inc(ada_rows_sb, 1)
            dve.wait_ge(adaT_ps, 1)
            adaT = psum[:, 5, :].rearrange("p (c b v) -> p b c v", c=4, b=4)[:, :, :, 0:2]
            dve.tensor_tensor(ada[:].rearrange("p (b c) v -> p b c v", b=4), adaT,
                              bac[:].rearrange("p (b c) -> p b c", b=4).unsqueeze(3).to_broadcast([P, 4, 4, 2]),
                              ALU.add).then_inc(a1_ready, 1)
            dve.wait_ge(a1_ready, 1)
            dve.scalar_tensor_tensor(out=a1[:], in0=ada[:, KC:2 * KC, :], scalar=1.0,
                                     in1=ng0[:].unsqueeze(2).to_broadcast([P, KC, 2]),
                                     op0=ALU.add, op1=ALU.mult).then_inc(a1_ready, 1)
            dve.wait_ge(a1_ready, 2)
            for k in range(0, KC, 2):
                dve.wait_ge(xT_ps, k + 1)
                for v in range(2):
                    half = slice(v * SEQ, (v + 1) * SEQ)
                    ins = dve.tensor_scalar(hT[:, k, half], psum[:, k % 4, half], a1[:, k, v:v + 1],
                                            ada[:, k, v:v + 1], ALU.mult, ALU.add)
                ins.then_inc(hT_dve, 1)
            step = 0
            for cb in range(4):
                for k in range(KC):
                    i = cb * KC + k
                    dve.wait_ge(ring_in[i % RING], 16 * (i // RING + 1))
                    if k == 0:
                        if cb >= 1:
                            dve.wait_ge(ada_sum_ps, cb)
                        ins = dve.tensor_scalar(ada_acc, ring[i % RING], silu[:, k, 0:1], None, ALU.mult)
                    else:
                        dve.wait_ge(ada_step, step)
                        ins = dve.scalar_tensor_tensor(out=ada_acc, in0=ring[i % RING], scalar=silu[:, k, 0:1],
                                                       in1=ada_acc, op0=ALU.mult, op1=ALU.add)
                    ins.then_inc(ada_step, 1)
                    step += 1
                if cb == 0:
                    dve.wait_ge(bada_in, 64)
                dve.wait_ge(ada_step, step)
                one = ada_acc[32 * cb:32 * cb + 1, :]
                dve.tensor_tensor(one, one, bada_rows[32 * cb:32 * cb + 1, :], ALU.add).then_inc(ada_step, 1)
                step += 1
                dve.wait_ge(ada_sum_ps, cb + 1)
                total = psum[:, 6:8, :].rearrange("p b n -> p (b n)")
                if cb == 0:
                    dve.wait_ge(rows_in, 48)
                    ins = dve.tensor_tensor(g1_row, total, g1_row, ALU.mult)
                elif cb == 1:
                    ins = dve.tensor_copy(sh2_row, total)
                elif cb == 2:
                    ins = dve.scalar_tensor_tensor(out=a2_row, in0=total, scalar=1.0, in1=a2_row,
                                                   op0=ALU.add, op1=ALU.mult)
                else:
                    ins = dve.tensor_tensor(g2_row[:], total, g2_row[:], ALU.mult)
                ins.then_inc(rows_ready, 1)

            for i in range(HEADS + 1):
                if i >= 1:
                    h = i - 1
                    dve.wait_ge(probs_ready, 2 * (h + 1))
                    dve.reciprocal(rsum[:, h, :], psumexp[:, h, :]).then_inc(rsum_ready, 1)
                    dve.wait_ge(rsum_ready, h + 1)
                    for t in range(TT):
                        ins = dve.tensor_scalar(probs[h % 2][:, t, :], probs[h % 2][:, t, :], rsum[:, h, t:t + 1],
                                                None, ALU.mult)
                    ins.then_inc(norm_ready, 1)
                if i < HEADS:
                    h = i
                    dve.wait_ge(scores_ps, h + 1)
                    dve.tensor_reduce(negmax[:, h, :], psum[:, 2 * (h % 2):2 * (h % 2) + 2, :], AX.X, ALU.max,
                                      negate=True).then_inc(negmax_ready, 1)
                if i >= 1:
                    h = i - 1
                    dve.wait_ge(probsT_ps, h + 1)
                    if h >= 2:
                        dve.wait_ge(pv_ps, h // 2)
                    dve.tensor_copy(probsT[h % 2].rearrange("p k n -> p (k n)"),
                                    psum[:, 4:6, :].rearrange("p b n -> p (b n)")).then_inc(probsT_sb, 1)
            inverse_deviation(2, TA + 2, 4, 6)
            for t in range(TT):
                dve.scalar_tensor_tensor(out=scaled[:, t, :], in0=psum[:, 4 + 2 * t:6 + 2 * t, :].rearrange("p b n -> p (b n)"),
                                         scalar=rstd[:, 4 + t:5 + t], in1=g1_row, op0=ALU.mult,
                                         op1=ALU.mult).then_inc(res_step, 1)
                dve.wait_ge(res_step, t + 1)
                dve.tensor_tensor(x_sb[:, t, :], scaled[:, t, :], x_sb[:, t, :], ALU.add).then_inc(x1_ready, 1)
            inverse_deviation(3, TA + 4, 6, 8)
            dve.wait_ge(bgu_step, 6)
            for t in range(TT):
                dve.wait_ge(x1_ready, t + 1)
                dve.scalar_tensor_tensor(out=scaled[:, t, :], in0=x_sb[:, t, :], scalar=rstd[:, 6 + t:7 + t],
                                         in1=a2_row, op0=ALU.mult, op1=ALU.mult).then_inc(res_step, 1)
                dve.wait_ge(res_step, TT + t + 1)
                dve.tensor_tensor(h2[:, t, :], scaled[:, t, :], sh2_row, ALU.add).then_inc(h2_ready, 1)
            for k in range(0, KC, 2):
                dve.wait_ge(h2T_ps, k + 1)
                dve.tensor_copy(h2T[:, k, :], psum[:, k % 4, 0:SEQ]).then_inc(h2T_dve, 1)

            steps = [1]

            def routed(ins):
                steps[0] += 1
                ins.then_inc(route_step, 1)
                dve.wait_ge(route_step, steps[0] - 1)

            dve.wait_ge(logits_ps, 1)
            dve.wait_ge(tables_in, 32)
            routed(dve.tensor_tensor(logits, psum[:, 4, 0:TT * E].rearrange("p (t e) -> p t e", t=TT),
                                     br_sb[:].unsqueeze(1).to_broadcast([P, TT, E]), ALU.add))
            for t in range(TT):
                routed(dve.max(top8[:, t, :], logits[:, t, :]))
                routed(dve.max_index(idx8[:, t, :], top8[:, t, :], logits[:, t, :]))
            dve.tensor_scalar(ntop[:], top8[:, :, 0], -1.0, None, ALU.mult).then_inc(route, 1)
            routed(dve.tensor_copy(idxf[:], idx8[:]))
            for t in range(TT):
                routed(dve.tensor_tensor(eq[:, t], slot_no[:, 0:E].unsqueeze(1).to_broadcast([P, TOPK, E]),
                                         idxf[:, t, 0:TOPK].unsqueeze(2).to_broadcast([P, TOPK, E]), ALU.is_equal))
                dve.tensor_reduce(member[:, t, :], eq[:, t].rearrange("p k e -> p e k"), AX.X,
                                  ALU.add).then_inc(member_ready, 1)
            dve.wait_ge(top_exp, TT)
            routed(dve.reciprocal(e4r[:], e4s[:]))
            routed(dve.tensor_tensor(g4[:], e4[:], e4r[:].unsqueeze(2).to_broadcast([P, TT, TOPK]), ALU.mult))
            for t in range(TT):
                routed(dve.tensor_tensor(geq[:, t], eq[:, t], g4[:, t, :].unsqueeze(2).to_broadcast([P, TOPK, E]),
                                         ALU.mult))
                dve.tensor_reduce(gates[:, t, :], geq[:, t].rearrange("p k e -> p e k"), AX.X,
                                  ALU.add).then_inc(gates_ready, 1)
            dve.wait_ge(pos_ps, 1)
            dve.wait_ge(member_ready, TT)
            routed(dve.scalar_tensor_tensor(out=pos[:], in0=psum[:, 5, 0:TT * E].rearrange("p (t e) -> p t e", t=TT),
                                            scalar=1.0, in1=member, op0=ALU.add, op1=ALU.mult))
            routed(dve.tensor_scalar(pos[:], pos[:], -1.0, None, ALU.add))
            counts = psum[0:1, 5, 2 * E:3 * E]
            routed(dve.tensor_scalar(nblk[:], counts, float(SLOTS), 1.0, ALU.is_gt, ALU.add))
            for more in range(2, SEQ // SLOTS):
                routed(dve.scalar_tensor_tensor(out=nblk[:], in0=counts, scalar=float(more * SLOTS), in1=nblk[:],
                                                op0=ALU.is_gt, op1=ALU.add))
            routed(dve.memset(one_row[:], 1.0))
            routed(dve.memset(cum[:, 0:1], 0.0))
            routed(dve.tensor_tensor_scan(cum[:, 1:E + 1], one_row[:], nblk[:], 0.0, ALU.mult, ALU.add))
            routed(dve.tensor_copy(first_block[:], cum[:]))
            dve.wait_ge(gatesT_ps, 1)
            dve.tensor_copy(gatesT, psum[0:E, 6, 0:SEQ]).then_inc(gatesT_sb, 1)
            dve.memset(y_sb, 0.0).then_inc(y_ready, 1)
            dve.memset(selT, 0.0).then_inc(selT_sb, 1)
            dve.memset(one_row[:], 1.0).then_inc(slots_used, COUNTED)
            dve.wait_ge(bdown_ps, 1)
            for t in range(TT):
                for h in range(2):
                    dve.tensor_copy(acc[:, t, h * BANK:(h + 1) * BANK], psum[:, 2 * t + h, :]).then_inc(comb_taken, 1)
            dve.wait_ge(comb_taken, 4)
            dve.wait_ge(selT_sb, 1)
            dve.wait_ge(y_ready, 1)
            dve.wait_ge(route_step, steps[0] - 1)
            dve.memset(one_row[:], 1.0).then_inc(blocks_ready, 1)

            def add_rows(g, part):
                for n in part:
                    t, h = n // 2, n % 2
                    a = acc[:, t, h * BANK:(h + 1) * BANK]
                    dve.wait_ge(comb_ps, 4 * g + n + 1)
                    dve.wait_ge(comb_taken, 4 * g + n + 1)
                    dve.tensor_tensor(a, psum[:, COMB + h, :], a, ALU.add).then_inc(comb_taken, 1)

            with dve.Fori(0, E) as e:
                g_first = dve.value_load(first_block[0:1, bass.ds(e, 1)], min_val=0, max_val=4 * E)
                g_end = dve.value_load(first_block[0:1, bass.ds(e + 1, 1)], min_val=1, max_val=4 * E)
                with dve.Fori(g_first, g_end) as g:
                    j0 = nc.s_assert_within((g - g_first) * SLOTS, 0, SEQ - SLOTS,
                                            skip_runtime_bounds_check_because="an expert has at most SEQ / SLOTS blocks")
                    for t in range(TT):
                        dve.tensor_scalar(sel[:, t, :], slot_no[:, bass.ds(j0, SLOTS)], pos[:, t, bass.ds(e, 1)],
                                          None, ALU.is_equal)
                        dve.tensor_scalar(sel_gate[:, t], slot_no[:, bass.ds(j0, SLOTS)].unsqueeze(1)
                                          .to_broadcast([P, 2, SLOTS]), pos[:, t, bass.ds(e, 1)],
                                          gates[:, t, bass.ds(e, 1)], ALU.is_equal, ALU.mult)
                    dve.tensor_scalar(pick[:], expert_no[:].to_broadcast([3 * E, SLOTS]),
                                      slot_no[0:3 * E, bass.ds(e, 1)], None, ALU.is_equal).then_inc(sel_ready, 1)
                    add_rows(g, (0, 1))
                    dve.wait_ge(gu_ps, 2 * g + 1)
                    dve.tensor_scalar(gate_sb, psum[:, GATE, :], LIMIT, None, ALU.min).then_inc(swiglu, 1)
                    dve.wait_ge(gu_ps, 2 * g + 2)
                    dve.tensor_scalar(up_sb, psum[:, UP, :], LIMIT, -LIMIT, ALU.min, ALU.max).then_inc(swiglu, 1)
                    dve.wait_ge(sig_ready, g + 1)
                    dve.tensor_tensor(sig_sb, gate_sb, sig_sb, ALU.mult).then_inc(swiglu, 1)
                    dve.wait_ge(swiglu, 4 * g + 3)
                    dve.scalar_tensor_tensor(out=hid_sb, in0=up_sb, scalar=1.0, in1=sig_sb,
                                             op0=ALU.add, op1=ALU.mult).then_inc(swiglu, 1)
                    add_rows(g, (2, 3))
                    dve.wait_ge(selT_ps, g + 1)
                    dve.tensor_copy(selT, psum[:, SELB, 0:SEQ]).then_inc(selT_sb, 1)
            total = dve.value_load(first_block[0:1, E:E + 1], min_val=1, max_val=4 * E)
            add_rows(total, range(4))
            for t in range(TT):
                dve.wait_ge(comb_taken, 4 * total + 8)
                dve.memset(ntop[:, t:t + 1], 0.0).then_inc(fin_step, 1)
            inverse_deviation(4, TA + 6, 8, 10)
            for t in range(TT):
                dve.scalar_tensor_tensor(out=acc[:, t, :], in0=acc[:, t, :], scalar=rstd[:, 8 + t:9 + t],
                                         in1=g2_row[:], op0=ALU.mult, op1=ALU.mult).then_inc(fin_step, 1)
                dve.wait_ge(fin_step, TT + t + 1)
                dve.tensor_tensor(h2[:, t, :], acc[:, t, :], x_sb[:, t, :], ALU.add).then_inc(fin_ready, 1)


def kernel(**inputs):
    import numpy as np
    import concourse.bacc as bacc
    from concourse.bass_utils import run_bass_kernel_spmd as run

    a = {n: np.asarray(v) for n, v in inputs.items()}

    def cols(v):
        return np.ascontiguousarray(np.moveaxis(v.reshape(v.shape[:-1] + (-1, P)), -1, 0))

    host = {
        "x": a["x"],
        "c_cols": np.ascontiguousarray(np.stack([cols(a["c"][0]), cols(a["c_ctx"])], axis=-1)),
        "ctx": a["ctx"],
        "w_ada": a["w_ada"],
        "b_ada_cols": cols(a["b_ada"][0, 0:2 * D]),
        "b_ada": a["b_ada"],
        "norm_cols": cols(a["norm_g"][0, 0]),
        "norm_g": a["norm_g"],
        "w_qkv": a["w_qkv"],
        "w_o": a["w_o"],
        "rpb": a["rpb"],
        "w_router": a["w_router"],
        "b_router": a["b_router"],
        "w_gu": a["w_gu"][0],
        "b_gu": a["b_gu"][0],
        "w_down": a["w_down"][0],
        "b_down": a["b_down"],
    }
    nc = bacc.Bacc("TRN2", target_bir_lowering=False, num_devices=1)
    arrays, args = {}, []
    for name, v in host.items():
        arrays[f"in_{name}"] = np.ascontiguousarray(v)
        args.append(nc.dram_tensor(f"in_{name}", v.shape, F32, kind="ExternalInput").ap())
    out = nc.dram_tensor("out_0", (1, SEQ, D), F32, kind="ExternalOutput").ap()
    build(nc, *args, out)
    r = run(nc, [arrays], core_ids=[0])
    return r.results[0]["out_0"]
```

```python
import math
from contextlib import ExitStack

import concourse.bass as bass
from concourse import mybir

F32 = mybir.dt.float32
F32R = mybir.dt.float32r
BF16 = mybir.dt.bfloat16
I32 = mybir.dt.int32
U32 = mybir.dt.uint32
ALU = mybir.AluOpType
ACT = mybir.ActivationFunctionType
AX = mybir.AxisListType

P = 128
D = 1024
KC = D // P
SEQ = 256
CTX = 256
TT = SEQ // P
TA = (SEQ + CTX) // P
KEYS = SEQ + CTX
HEADS = 16
HD = D // HEADS
GRID_W = 64
WIN_ROWS, WIN_COLS = 8, 16
RPB_R, RPB_C = 2 * WIN_ROWS - 1, 2 * WIN_COLS - 1
ROWS = SEQ // GRID_W
BROWS = ROWS + 2
E = 32
TOPK = 4
EPS = 1e-6
LIMIT = 7.0
ALPHA = 1.702
MASKED = -1e30
SLOTS = 32
PARTS = P // SLOTS
PW = D // PARTS
PC = PW // P
BLOCKS = E + TOPK * SEQ // SLOTS
BANK = 512
GU = 2 * D
UNIT = GU
UNITS = 12
PLACES = 20
CYCLE = PLACES // math.gcd(PLACES, UNITS)
UC = D // P
RING = 4
STEPS = 4 * KC // 2


def build(nc, x, c_cols, ctx, w_ada, b_ada_cols, b_ada, norm_cols, norm_g, w_qkv, w_o, rpb,
          w_router, b_router, w_gu, b_gu, w_down, b_down, out):
    with ExitStack() as stack:
        def sb(name, shape, dt=F32):
            return stack.enter_context(nc.sbuf_tensor(name, shape, dt))

        def sem(name):
            return stack.enter_context(nc.semaphore(name))

        psum = stack.enter_context(nc.psum_tensor("psum", [P, 8, BANK], F32))

        with ExitStack() as first:
            w_lo_r, hT_hi_r, v_hi_r, hT_lo_r, _, k_hi_r = (
                first.enter_context(nc.sbuf_tensor(name, [P, words], F32R)) for name, words in
                (("w_lo_r", 16 * D), ("hT_hi_r", 4 * D), ("v_hi_r", 4 * D),
                 ("hT_lo_r", 4 * D), ("between_r", 4 * D), ("k_hi_r", 4 * D)))

        warena = sb("warena", [P, 2 * 6 * UNIT])
        dn0 = KC * UNIT
        ada_slot = [warena[:, k * UNIT:(k + 1) * UNIT] for k in range(KC)]
        q_words = KC * BANK
        qkv_at = [dn0, dn0 + q_words] + [b * q_words for b in range(4)]
        qkv_blk = [warena[:, a:a + q_words].rearrange("p (k n) -> p k n", k=KC) for a in qkv_at]
        bias = warena[:, 0:HEADS * BROWS * GRID_W].rearrange("p (h r w) -> p h r w", h=HEADS, r=BROWS)
        wo_sb = warena[:, KC * D:2 * KC * D].rearrange("p (k n) -> p k n", k=KC)

        parena = sb("parena", [P, 14 * D])
        hT = parena[:, 0:4 * D].rearrange("p (k n) -> p k n", k=KC)
        xn = parena[:, 4 * D:8 * D].rearrange("p (t n) -> p t n", t=TA)
        kT = parena[:, 4 * D:8 * D].rearrange("p (k n) -> p k n", k=KC)
        v_sb = parena[:, 8 * D:12 * D].rearrange("p (t n) -> p t n", t=TA)
        qT = parena[:, 12 * D:14 * D].rearrange("p (k n) -> p k n", k=KC)
        oT = parena[:, 2 * D:4 * D].rearrange("p (k n) -> p k n", k=KC)
        acc = parena[:, 12 * D:14 * D].rearrange("p (t n) -> p t n", t=TT)
        h2T = parena[:, 2 * D:4 * D].rearrange("p (k n) -> p k n", k=KC)
        bd_sb = parena[0:E, 12 * D:13 * D]
        eq, geq = (parena[:, 13 * D + i * 256:13 * D + (i + 1) * 256]
                   .rearrange("p (t k e) -> p t k e", t=TT, k=TOPK) for i in range(2))

        hT_hi_r, hT_lo_r = (a[:].rearrange("p (k n) -> p k n", k=KC) for a in (hT_hi_r, hT_lo_r))

        def w_hi(s):
            a = k_hi_r if s < STEPS // 2 else v_hi_r
            return a[:, (s % 4) * D:(s % 4 + 1) * D].rearrange("p (k n) -> p k n", k=2)

        def w_raw(s, place=warena):
            a = qkv_at[2 + s // 4] + 2 * (s % 4) * BANK
            return place[:, a:a + 2 * BANK].rearrange("p (k n) -> p k n", k=2)

        x_sb = sb("x_sb", [P, TT, D])
        h2 = sb("h2", [P, TT, D])
        ctx_sb = h2
        ring2 = h2[:].rearrange("p t n -> p (t n)")
        g2_row = sb("g2_row", [P, D])

        work = sb("work", [P, 3 * D + 2 * UNIT])
        g1_row, sh2_row, a2_row = (work[:, i * D:(i + 1) * D] for i in range(3))
        ada_acc = work[:, 3 * D:4 * D]
        ada_rows = work[:, 3 * D:3 * D + BANK]
        ring = [ring2[:, 0:D], ring2[:, D:2 * D], work[:, 4 * D:5 * D], work[:, 5 * D:6 * D]]
        probs = [work[:, (3 + i) * D:(4 + i) * D].rearrange("p (t n) -> p t n", t=TT) for i in range(2)]
        square = work[:, 5 * D:6 * D]
        scaled = work[:, 3 * D:5 * D].rearrange("p (t n) -> p t n", t=TT)
        probsT = [a.rearrange("p (k n) -> p k n", k=TA) for a in (work[:, 5 * D:6 * D], parena[:, 0:D])]
        xg_sb, gate_sb, up_sb, sig_sb, hid_sb, y_sb = (work[:, i * PW:(i + 1) * PW] for i in range(6))
        xgT, hidT = (work[:, i * PW:(i + 1) * PW].rearrange("p (c q s) -> p c q s", c=PC, q=PARTS)
                     for i in (6, 7))
        sel = work[:, 11 * PW:11 * PW + TT * SLOTS].rearrange("p (t s) -> p t s", t=TT)
        sel_gate = work[:, 10 * PW:10 * PW + TT * P].rearrange("p (t q s) -> p t q s", t=TT, q=PARTS)
        selT = work[:, 9 * PW:9 * PW + SEQ]
        bgu_raw = ring2[0:3 * E, :]
        bgu3_all = sb("bgu3", [P, GU], BF16)
        bgu3 = bgu3_all[0:3 * E, :]
        bada_rows = bgu3_all[:].bitcast(F32)
        expert_no = sb("expert_no", [3 * E, 1])
        pick = sb("pick", [3 * E, SLOTS], BF16)

        wr_sb = parena[:, 13 * D + 256:13 * D + 512].rearrange("p (k e) -> p k e", k=KC)
        early_at = [6 * D]

        def early(*shape):
            words = math.prod(shape)
            early_at[0] += words
            a = work[:, early_at[0] - words:early_at[0]]
            if len(shape) == 1:
                return a
            return a.rearrange("p (a b) -> p a b", a=shape[0])

        br_sb = early(E)
        ident = sb("ident", [P, P])
        flip = early(P)
        before = early(P)
        ones = sb("ones", [P, P])
        slot_no = sb("slot_no", [P, SEQ])
        c_sb = early(KC, 2)
        csig = early(KC, 2)
        silu = early(KC, 32)
        bac = early(2 * KC)
        ng0 = early(KC)
        ada = early(2 * KC, 2)
        a1 = early(KC, 2)
        ss = sb("ss", [P, 12])
        var = sb("var", [P, 12])
        std = sb("std", [P, 12])
        rstd = sb("rstd", [P, 12])
        negmax = early(HEADS, TT)
        psumexp = early(HEADS, TT)
        rsum = early(HEADS, TT)
        logits = parena[:, 13 * D + 768:13 * D + 768 + TT * E].rearrange("p (t e) -> p t e", t=TT)
        top8 = sb("top8", [P, TT, 8])
        idx8 = sb("idx8", [P, TT, 8], U32)
        idxf = sb("idxf", [P, TT, 8])
        ntop = sb("ntop", [P, TT])
        e4 = sb("e4", [P, TT, TOPK])
        e4s = sb("e4s", [P, TT])
        e4r = sb("e4r", [P, TT])
        g4 = sb("g4", [P, TT, TOPK])
        member = parena[:, 13 * D + 896:13 * D + 896 + TT * E].rearrange("p (t e) -> p t e", t=TT)
        gates = sb("gates", [P, TT, E])
        gatesT = parena[0:E, 13 * D + 512:13 * D + 512 + SEQ]
        pos = sb("pos", [P, TT, E])
        nblk = sb("nblk", [1, E])
        one_row = sb("one_row", [1, E])
        cum = sb("cum", [1, E + 1])
        first_block = sb("first_block", [1, E + 1], I32)

        x_in, ctx_in, consts_in, tables_in, rows_in, wo_in, out_done = (
            sem(n) for n in ("x_in", "ctx_in", "consts_in", "tables_in", "rows_in", "wo_in", "out_done"))
        ada_in = [sem(f"ada_in{k}") for k in range(KC)]
        qkv_in = [sem(f"qkv_in{b}") for b in range(6)]
        ring_in = [sem(f"ring_in{r}") for r in range(RING)]
        bias_in = [sem(f"bias_in{a}") for a in range(2)]
        bada_in, bdown_in = sem("bada_in"), sem("bdown_in")
        const_ready, bias_masked = sem("const_ready"), sem("bias_masked")
        csig_ready, silu_ready = sem("csig_ready"), sem("silu_ready")
        squares, vars_ready, std_ready, rstd_ready, xn_ready = (
            sem(n) for n in ("squares", "vars_ready", "std_ready", "rstd_ready", "xn_ready"))
        ada_used, ada_ready, a1_ready = sem("ada_used"), sem("ada_ready"), sem("a1_ready")
        xT_ps, xT_dve, xT_act, hT_dve, hT_act = (
            sem(n) for n in ("xT_ps", "xT_dve", "xT_act", "hT_dve", "hT_act"))
        proj_ps, proj_sb = sem("proj_ps"), sem("proj_sb")
        hT_hi_ready, hT_lo_ready, w_hi_ready, w_lo_ready, w_used = (
            sem(n) for n in ("hT_hi_ready", "hT_lo_ready", "w_hi_ready", "w_lo_ready", "w_used"))
        ada_step, ada_sum_ps, rows_ready = sem("ada_step"), sem("ada_sum_ps"), sem("rows_ready")
        scores_ps, negmax_ready, probs_ready = sem("scores_ps"), sem("negmax_ready"), sem("probs_ready")
        probsT_ps, probsT_sb, pv_ps, rsum_ready = (
            sem(n) for n in ("probsT_ps", "probsT_sb", "pv_ps", "rsum_ready"))
        oT_ready, attn_out_ps, norm_ready = sem("oT_ready"), sem("attn_out_ps"), sem("norm_ready")
        bgu_in, bgu_step, adaT_ps, ada_rows_ps, ada_rows_sb = (
            sem(n) for n in ("bgu_in", "bgu_step", "adaT_ps", "ada_rows_ps", "ada_rows_sb"))
        res_step, x1_ready, h2_ready = sem("res_step"), sem("x1_ready"), sem("h2_ready")
        h2T_ps, h2T_dve, h2T_act, logits_ps = sem("h2T_ps"), sem("h2T_dve"), sem("h2T_act"), sem("logits_ps")
        route_step = sem("route_step")
        route, top_exp, member_ready, gates_ready, pos_ps = (
            sem(n) for n in ("route", "top_exp", "member_ready", "gates_ready", "pos_ps"))
        gatesT_ps, gatesT_sb, bdown_ps, blocks_ready = (
            sem(n) for n in ("gatesT_ps", "gatesT_sb", "bdown_ps", "blocks_ready"))
        unit_in = [sem(f"unit_in{u}") for u in range(UNITS)]
        units_used, sel_ready, selT_ps, selT_sb = (
            sem(n) for n in ("units_used", "sel_ready", "selT_ps", "selT_sb"))
        xg_ps, xg_sb_ready, gu_ps, swiglu, sig_ready = (
            sem(n) for n in ("xg_ps", "xg_sb_ready", "gu_ps", "swiglu", "sig_ready"))
        xgT_ps, xgT_sb, hidT_ps, hidT_sb = (sem(n) for n in ("xgT_ps", "xgT_sb", "hidT_ps", "hidT_sb"))
        y_ps, y_ready, comb_ps, comb_taken = (
            sem(n) for n in ("y_ps", "y_ready", "comb_ps", "comb_taken"))
        fin_step, fin_ready = sem("fin_step"), sem("fin_ready")

        block = stack.enter_context(nc.Block())
        last_comb = (4, 0)
        SUM_AFTER = (0, 3, 6, 10)
        SPLITS_AT = {(0, 4): range(4), (1, 2): (4,), (1, 5): (5,), (2, 0): (6,), (2, 2): (7,), (2, 4): (8,),
                     (2, 6): (9,), (3, 3): (10,), (3, 6): (11,)}
        N_CONST = 12
        COUNTED = UNITS - 2
        XG_SEL, TURN, GATE_UP, YB, COMB = 0, 1, 2, 3, 4
        xg_at, selT_at = psum[:, XG_SEL, 0:PW], psum[:, XG_SEL, PW:PW + SEQ]
        turn_at, y_at = psum[:, TURN, 0:PW], psum[:, YB, 0:PW]

        def unit_at(start, u):
            n = (start + u) % PLACES
            for arena, places in ((warena, UNITS), (parena, 6), (work[:, 3 * D:], 2)):
                if n < places:
                    return arena[:, n * UNIT:(n + 1) * UNIT]
                n -= places

        def load_unit(sp, e, start, u):
            ex = bass.ds(e, 1)
            if u < KC:
                src = w_gu[ex, u * P:(u + 1) * P, :].rearrange("o p n -> (o p) n")
                dst = unit_at(start, u)
            else:
                f = 2 * (u - KC)
                src = w_down[ex, f * P:(f + 2) * P, :].rearrange("o (c p) n -> (o p) c n", c=2)
                dst = unit_at(start, u).rearrange("p (c n) -> p c n", c=2)
            sp.dma_start(dst, src).then_inc(unit_in[u], 16)

        def wait_unit_used(sp, u, blocks):
            if u == KC - 1:
                sp.wait_ge(gu_ps, blocks)
            elif u == UNITS - 1:
                sp.wait_ge(y_ps, blocks)
            else:
                sp.wait_ge(units_used, COUNTED * blocks + (u + 1 if u < KC else u))

        @block.sync
        def _(sp):
            sp.dma_start(c_sb, c_cols).then_inc(consts_in, 16)
            sp.dma_start(bac, b_ada_cols).then_inc(consts_in, 16)
            sp.dma_start(ng0, norm_cols).then_inc(consts_in, 16)
            sp.dma_start(x_sb[:], x[0].rearrange("(t p) n -> p t n", p=P)).then_inc(x_in, 16)
            sp.dma_start(ctx_sb[:], ctx[0].rearrange("(t p) n -> p t n", p=P)).then_inc(ctx_in, 16)
            for k in range(KC):
                sp.dma_start(ada_slot[k], w_ada[0, k * P:(k + 1) * P, 0:2 * D]).then_inc(ada_in[k], 16)
            for i in range(4):
                sp.dma_start(bada_rows[32 * i:32 * i + 1, :], b_ada[0:1, (2 + i) * D:(3 + i) * D]).then_inc(bada_in, 16)
            wq = w_qkv[0].rearrange("(k p) n -> p k n", p=P)
            for b in range(6):
                if b >= 2:
                    sp.wait_ge(ada_used, 2 * (b - 1))
                    sp.wait_ge(ada_step, (2, 6, 14, 23)[b - 2])
                sp.dma_start(qkv_blk[b], wq[:, :, b * BANK:(b + 1) * BANK]).then_inc(qkv_in[b], 16)
            sp.dma_start(br_sb, b_router.to_broadcast([P, E])).then_inc(tables_in, 16)
            sp.wait_ge(proj_ps, 16)
            for a in range(2):
                if a == 1:
                    sp.wait_ge(ada_step, 4 * (KC + 1) - 1 - RING)
                for r in range(BROWS):
                    row = WIN_ROWS - 1 - 2 - a + r
                    src = bass.AP(tensor=rpb.tensor, offset=row * RPB_C + WIN_COLS - 1 - (GRID_W - 1),
                                  ap=[[1, GRID_W], [RPB_R * RPB_C, HEADS], [1, GRID_W]])
                    sp.dma_start(bias[GRID_W * a:GRID_W * (a + 1), :, r, :], src).then_inc(bias_in[a], 16)
            load_unit(sp, 0, 0, 3)
            sp.wait_ge(proj_ps, 24)
            sp.dma_start(wo_sb, w_o[0].rearrange("(k p) n -> p k n", p=P)).then_inc(wo_in, 16)
            for u in range(KC, UNITS):
                load_unit(sp, 0, 0, u)
            sp.wait_ge(rows_ready, 4)
            for part in range(3):
                sp.dma_start(bgu_raw[part * E:(part + 1) * E, :], b_gu).then_inc(bgu_in, 16)
            sp.wait_ge(scores_ps, HEADS)
            sp.dma_start(wr_sb, w_router[0].rearrange("(k p) e -> p k e", p=P)).then_inc(tables_in, 16)
            for u in range(3):
                load_unit(sp, 0, 0, u)
            sp.wait_ge(attn_out_ps, TT)
            sp.dma_start(bd_sb, b_down[0]).then_inc(bdown_in, 16)
            for u in range(4, KC):
                load_unit(sp, 0, 0, u)

            for u in (0, *range(2, 6), 1, 6, 7):
                if u == 1:
                    sp.wait_ge(logits_ps, 1)
                if u == 7:
                    sp.wait_ge(pos_ps, 1)
                sp.wait_ge(unit_in[u], 16)
                load_unit(sp, 1, UNITS, u)

            def load_expert(e, start, units):
                before_last = sp.value_load(first_block[0:1, bass.ds(e - 1, 1)], min_val=0, max_val=BLOCKS)
                last = sp.value_load(first_block[0:1, bass.ds(e, 1)], min_val=1, max_val=BLOCKS)
                for u in units:
                    if u < PLACES - UNITS:
                        wait_unit_used(sp, u + 2 * UNITS - PLACES, before_last)
                    else:
                        wait_unit_used(sp, u - (PLACES - UNITS), last)
                    sp.wait_ge(unit_in[u], landed)
                    load_unit(sp, e, start, u)
                sp.reg_add(landed, landed, 16)

            landed = sp.alloc_register("landed")
            sp.reg_mov(landed, 16)
            sp.wait_ge(blocks_ready, 1)
            load_expert(1, UNITS, range(PLACES - UNITS, UNITS))
            with sp.Fori(0, (E - 2) // CYCLE) as i:
                for r in range(2, CYCLE + 2):
                    load_expert(sp.snap(CYCLE * i + r), UNITS * r % PLACES, range(UNITS))
            for t in range(TT):
                sp.wait_ge(fin_ready, t + 1)
                sp.dma_start(out[0, t * P:(t + 1) * P, :], h2[:, t, :]).then_inc(out_done, 16)
            sp.wait_ge(out_done, 16 * TT)

        @block.gpsimd
        def _(pool):
            made = 0

            def make(ins):
                nonlocal made
                made += 1
                ins.then_inc(const_ready, 1)
                pool.wait_ge(const_ready, made)

            make(pool.memset(ident[:], 0.0))
            make(pool.memset(flip, 0.0))
            make(pool.memset(before, 1.0))
            make(pool.memset(ones[:], 1.0))
            make(pool.affine_select(out=ident[:], in_=ident[:], compare_op=ALU.not_equal, fill=1.0, base=0,
                                    pattern=[[-1, P]], channel_multiplier=1))
            for a in range(2):
                blk = flip[GRID_W * a:GRID_W * (a + 1), GRID_W * a:GRID_W * (a + 1)]
                make(pool.affine_select(out=blk, in_=blk, compare_op=ALU.not_equal, fill=1.0, base=-(GRID_W - 1),
                                        pattern=[[1, GRID_W]], channel_multiplier=1))
            make(pool.affine_select(out=before, in_=before, compare_op=ALU.is_gt, fill=0.0, base=0,
                                    pattern=[[1, P]], channel_multiplier=-1))
            make(pool.iota(slot_no[:], pattern=[[1, SEQ]], base=0, channel_multiplier=0,
                           allow_small_or_imprecise_dtypes=True))
            for part in range(3):
                make(pool.iota(expert_no[part * E:(part + 1) * E, :], pattern=[[0, 1]], base=0, channel_multiplier=1,
                               allow_small_or_imprecise_dtypes=True))
            for i in range(4 * KC):
                cb, k = i // KC, i % KC
                if i == 0:
                    pool.wait_ge(xn_ready, TA)
                    pool.wait_ge(ada_used, KC - 1)
                if i >= RING:
                    last = i - RING
                    pool.wait_ge(ada_step, (KC + 1) * (last // KC) + last % KC + 1)
                pool.dma_start(ring[i % RING], w_ada[0, k * P:(k + 1) * P, (2 + cb) * D:(3 + cb) * D]) \
                    .then_inc(ring_in[i % RING], 16)
                if i == 2 * RING - 1:
                    for n, row in ((1, g1_row), (2, a2_row), (3, g2_row[:])):
                        pool.dma_start(row, norm_g[0, n:n + 1, :].to_broadcast([P, D])).then_inc(rows_in, 16)
            for a in range(2):
                pool.wait_ge(bias_in[a], 16 * BROWS)
                tab = bias[GRID_W * a:GRID_W * (a + 1)].rearrange("p h r w -> p (h r) w")
                lo = tab[:, :, 0:GRID_W - WIN_COLS]
                hi = tab[:, :, WIN_COLS:GRID_W]
                n = GRID_W - WIN_COLS
                pool.affine_select(out=lo, in_=lo, compare_op=ALU.is_ge, fill=MASKED,
                                   base=WIN_COLS // 2 - (GRID_W - 1), pattern=[[0, HEADS * BROWS], [1, n]],
                                   channel_multiplier=1).then_inc(bias_masked, 1)
                pool.wait_ge(bias_masked, 2 * a + 1)
                pool.affine_select(out=hi, in_=hi, compare_op=ALU.is_ge, fill=MASKED,
                                   base=GRID_W - 1 + WIN_COLS // 2 - 1 - WIN_COLS,
                                   pattern=[[0, HEADS * BROWS], [-1, n]],
                                   channel_multiplier=-1).then_inc(bias_masked, 1)
                pool.wait_ge(bias_masked, 2 * a + 2)
            pool.wait_ge(bgu_in, 48)
            split = 0

            def part_of(ins):
                nonlocal split
                split += 1
                ins.then_inc(bgu_step, 1)
                pool.wait_ge(bgu_step, split)

            part_of(pool.tensor_copy(bgu3, bgu_raw))
            part_of(pool.tensor_tensor(bgu_raw, bgu_raw, bgu3, ALU.subtract))
            part_of(pool.tensor_copy(bgu3[E:2 * E, :], bgu_raw[E:2 * E, :]))
            third = slice(2 * E, 3 * E)
            part_of(pool.tensor_copy(bgu3[third, :], bgu_raw[third, :]))
            part_of(pool.tensor_tensor(bgu_raw[third, :], bgu_raw[third, :], bgu3[third, :], ALU.subtract))
            part_of(pool.tensor_copy(bgu3[third, :], bgu_raw[third, :]))

        @block.tensor
        def _(pe):
            pe.wait_ge(const_ready, N_CONST)
            pe.wait_ge(silu_ready, 2)
            def turn_tokens(k):
                if k == 0:
                    pe.wait_ge(xn_ready, TA)
                if k >= 4:
                    pe.wait_ge(xT_dve if k % 2 == 0 else xT_act, k // 2 - 1)
                for t in range(TA):
                    mm = pe.transpose(psum[:, k % 4, t * P:(t + 1) * P], xn[:, t, k * P:(k + 1) * P], ident[:])
                mm.then_inc(xT_ps, 1)

            for k in range(KC):
                pe.wait_ge(ada_in[k], 16)
                for b in range(4):
                    mm = pe.matmul(psum[32 * b:32 * (b + 1), 4, :], silu[:, k, :],
                                   ada_slot[k][:, b * BANK:(b + 1) * BANK], start=(k == 0), stop=(k == KC - 1))
                mm.then_inc(ada_used, 1)
                if 1 <= k < KC - 1:
                    turn_tokens(k - 1)
            turn_tokens(KC - 2)
            pe.wait_ge(ada_rows_sb, 1)
            for c in range(4):
                mm = pe.transpose(psum[:, 5, c * P:(c + 1) * P], ada_rows[:, c * P:(c + 1) * P], ident[:])
            mm.then_inc(adaT_ps, 1)
            turn_tokens(KC - 1)

            def ada_sum(cb):
                pe.wait_ge(ada_step, (KC + 1) * (cb + 1))
                if cb >= 1:
                    pe.wait_ge(rows_ready, cb)
                for h in range(2):
                    mm = pe.matmul(psum[:, 6 + h, :], ones[:], ada_acc[:, h * BANK:(h + 1) * BANK],
                                   start=True, stop=True)
                mm.then_inc(ada_sum_ps, 1)

            for n in range(8):
                blk, j = n // 4, n % 4
                if j == 0:
                    pe.wait_ge(qkv_in[blk], 16)
                if n >= 4:
                    pe.wait_ge(proj_sb, n - 3)
                for k in range(KC):
                    if n == 0:
                        pe.wait_ge(hT_dve if k % 2 == 0 else hT_act, k // 2 + 1)
                    mm = pe.matmul(psum[:, j, 0:SEQ], qkv_blk[blk][:, k, j * P:(j + 1) * P], hT[:, k, 0:SEQ],
                                   start=(k == 0), stop=(k == KC - 1))
                mm.then_inc(proj_ps, 1)
            for s in range(STEPS):
                blk = s // 4
                pe.wait_ge(w_hi_ready, s + 1)
                pe.wait_ge(w_lo_ready, s + 1)
                hi, lo = w_hi(s), w_raw(s, w_lo_r)
                for c in range(2):
                    k = 2 * (s % 4) + c
                    if blk == 0:
                        pe.wait_ge(hT_hi_ready, k + 1)
                        pe.wait_ge(hT_lo_ready, k + 1)
                    x_hi, x_lo = hT_hi_r[:, k, :], hT_lo_r[:, k, :]
                    for j in range(4):
                        if k == 0:
                            pe.wait_ge(proj_sb, 8 + 4 * blk + j - 3)
                        cols = slice(j * P, (j + 1) * P)
                        for i, (w, xx) in enumerate(((hi, x_hi), (hi, x_lo), (lo, x_hi))):
                            if blk < 2:
                                lhsT, rhs = w[:, c, cols], xx
                            else:
                                lhsT, rhs = xx[:, cols], w[:, c, :]
                            mm = pe.matmul(psum[:, j, :], lhsT, rhs, start=(k == 0 and i == 0),
                                           stop=(k == KC - 1 and i == 2))
                        if k == KC - 1:
                            mm.then_inc(proj_ps, 1)
                        elif j == 3 and c == 1:
                            mm.then_inc(w_used, 1)
                if s in SUM_AFTER:
                    ada_sum(SUM_AFTER.index(s))

            def scores(h):
                j, r = h // 2, HD * (h % 2)
                if h < 2:
                    pe.wait_ge(proj_sb, 24)
                    pe.wait_ge(bias_masked, 4)
                else:
                    pe.wait_ge(probs_ready, 2 * (h - 1))
                for t in range(TT):
                    s = psum[:, 2 * (h % 2) + t, :]
                    pe.matmul(s[:, 0:KEYS], qT[r:r + HD, j, t * P:(t + 1) * P], kT[r:r + HD, j, :],
                              start=True, stop=False)
                    mm = pe.matmul(s[:, 0:SEQ], flip,
                                   bias[:, h, 2 - 2 * t:2 - 2 * t + ROWS, :].rearrange("p r w -> p (r w)"),
                                   start=False, stop=True)
                mm.then_inc(scores_ps, 1)

            def turn_probs(h):
                pe.wait_ge(norm_ready, h + 1)
                if h >= 1:
                    pe.wait_ge(probsT_sb, h)
                for k in range(TA):
                    for t in range(TT):
                        o = (k % 2) * SEQ + t * P
                        mm = pe.transpose(psum[:, 4 + k // 2, o:o + P], probs[h % 2][:, t, k * P:(k + 1) * P], ident[:])
                mm.then_inc(probsT_ps, 1)

            def values(j):
                pe.wait_ge(probsT_sb, 2 * j + 2)
                if j < 2:
                    pe.wait_ge(rows_ready, 4)
                else:
                    pe.wait_ge(oT_ready, j - 1)
                for k in range(TA):
                    for o in range(2):
                        h = 2 * j + o
                        mm = pe.matmul(psum[o * HD:(o + 1) * HD, 6 + j % 2, 0:SEQ], v_sb[:, k, h * HD:(h + 1) * HD],
                                       probsT[o][:, k, :], start=(k == 0), stop=(k == TA - 1))
                mm.then_inc(pv_ps, 1)

            for i in range(HEADS + 2):
                if i < HEADS:
                    scores(i)
                if 1 <= i <= HEADS:
                    turn_probs(i - 1)
                if i >= 2 and i % 2 == 1:
                    values((i - 3) // 2)

            pe.wait_ge(oT_ready, KC)
            pe.wait_ge(wo_in, 16)
            for t in range(TT):
                for h in range(2):
                    for j in range(KC):
                        mm = pe.matmul(psum[:, 4 + 2 * t + h, :], oT[:, j, t * P:(t + 1) * P],
                                       wo_sb[:, j, h * BANK:(h + 1) * BANK], start=(j == 0), stop=(j == KC - 1))
                mm.then_inc(attn_out_ps, 1)

            for t in range(TT):
                pe.wait_ge(h2_ready, t + 1)
                for k in range(KC):
                    mm = pe.transpose(psum[:, 2 * t + k // 4, k % 4 * P:(k % 4 + 1) * P],
                                      h2[:, t, k * P:(k + 1) * P], ident[:])
                    if k % 4 == 3:
                        mm.then_inc(h2T_ps, 1)
                if t == 0:
                    pe.wait_ge(tables_in, 16 * 2)
                pe.wait_ge(h2T_dve, t + 1)
                pe.wait_ge(h2T_act, t + 1)
                for k in range(KC):
                    mm = pe.matmul(psum[:, 4, t * E:(t + 1) * E], h2T[:, k, t * P:(t + 1) * P], wr_sb[:, k, :],
                                   start=(k == 0), stop=(k == KC - 1))
            mm.then_inc(logits_ps, 1)
            pe.wait_ge(member_ready, TT)
            pe.matmul(psum[:, 5, 0:E], before, member[:, 0, :], start=True, stop=True)
            pe.matmul(psum[:, 5, E:2 * E], ones[:], member[:, 0, :], start=True, stop=False)
            pe.matmul(psum[:, 5, E:2 * E], before, member[:, 1, :], start=False, stop=True)
            pe.matmul(psum[:, 5, 2 * E:3 * E], ones[:], member[:, 0, :], start=True, stop=False)
            pe.matmul(psum[:, 5, 2 * E:3 * E], ones[:], member[:, 1, :], start=False, stop=True).then_inc(pos_ps, 1)
            pe.wait_ge(gates_ready, TT)
            for t in range(TT):
                mm = pe.transpose(psum[0:E, 6, t * P:(t + 1) * P], gates[:, t, :], ident[:])
            mm.then_inc(gatesT_ps, 1)
            pe.wait_ge(gatesT_sb, 1)
            pe.wait_ge(bdown_in, 16)
            pe.wait_ge(blocks_ready, 1)
            for t in range(TT):
                for h in range(2):
                    mm = pe.matmul(psum[:, COMB + 2 * t + h, :], gatesT[:, t * P:(t + 1) * P],
                                   bd_sb[:, h * BANK:(h + 1) * BANK], start=True, stop=True)
            mm.then_inc(bdown_ps, 1)

            def part_rows(q):
                return slice(q * SLOTS, (q + 1) * SLOTS)

            def combine(g, t, bank=COMB):
                if t == 0:
                    pe.wait_ge(y_ready, g + 1)
                    pe.wait_ge(selT_sb, g + 1)
                if bank == COMB:
                    pe.wait_ge(comb_taken, 2 * g + t + 2)
                for q in range(PARTS):
                    mm = pe.matmul(psum[:, bank + q, 0:PW], selT[part_rows(q), t * P:(t + 1) * P],
                                   y_sb[part_rows(q), :], start=True, stop=True)
                mm.then_inc(comb_ps, 1)

            pe.wait_ge(bgu_step, 6)

            gate_up = psum[:, GATE_UP, :].rearrange("p (b n) -> p b n", b=2)

            def gate_and_up(rows, q):
                return rows.rearrange("p (b n) -> p b n", b=2)[:, :, q * PW:(q + 1) * PW]

            def expert(e, start):
                unit = [unit_at(start, u) for u in range(UNITS)]
                g_first = pe.value_load(first_block[0:1, bass.ds(e, 1)], min_val=0, max_val=BLOCKS)
                g_end = pe.value_load(first_block[0:1, bass.ds(e + 1, 1)], min_val=1, max_val=BLOCKS)
                with pe.Fori(g_first, g_end) as g:
                    pe.wait_ge(sel_ready, g + 1)
                    pe.wait_ge(selT_sb, g + 1)
                    for t in range(TT):
                        mm = pe.transpose(selT_at[:, t * P:(t + 1) * P],
                                          sel_gate[:, t].rearrange("p q s -> p (q s)"), ident[:])
                    mm.then_inc(selT_ps, 1)
                    for t in range(TT):
                        for q in range(PARTS):
                            mm = pe.matmul(xg_at[part_rows(q), :], sel[:, t, :],
                                           h2[:, t, q * PW:(q + 1) * PW], start=(t == 0), stop=(t == TT - 1))
                    mm.then_inc(xg_ps, 1)
                    combine(g, 0)
                    pe.wait_ge(xg_sb_ready, g + 1)
                    for c in range(PC):
                        mm = pe.transpose(turn_at[:, c * P:(c + 1) * P], xg_sb[:, c * P:(c + 1) * P], ident[:])
                    mm.then_inc(xgT_ps, 1)
                    for q in range(PARTS):
                        pe.matmul(gate_up[part_rows(q)], pick[:], gate_and_up(bgu3, q), start=True, stop=False)
                    pe.wait_ge(xgT_sb, g + 1)
                    for k in range(KC):
                        pe.wait_ge(unit_in[k], 16 * e + 16)
                        for q in range(PARTS):
                            mm = pe.matmul(gate_up[part_rows(q)], xgT[:, k % PC, k // PC, :],
                                           gate_and_up(unit[k], q), start=False, stop=(k == KC - 1))
                        mm.then_inc(units_used if k < KC - 1 else gu_ps, 1)
                    combine(g, 1)
                    pe.wait_ge(swiglu, 4 * g + 4)
                    for c in range(PC):
                        mm = pe.transpose(turn_at[:, c * P:(c + 1) * P], hid_sb[:, c * P:(c + 1) * P], ident[:])
                    mm.then_inc(hidT_ps, 1)
                    pe.wait_ge(hidT_sb, g + 1)
                    for f in range(KC):
                        if f % 2 == 0:
                            pe.wait_ge(unit_in[KC + f // 2], 16 * e + 16)
                        for q in range(PARTS):
                            c0 = (f % 2) * D + q * PW
                            mm = pe.matmul(y_at[part_rows(q), :], hidT[:, f % PC, f // PC, :],
                                           unit[KC + f // 2][:, c0:c0 + PW], start=(f == 0), stop=(f == KC - 1))
                        if f == KC - 1:
                            mm.then_inc(y_ps, 1)
                        elif f % 2 == 1:
                            mm.then_inc(units_used, 1)
            with pe.Fori(0, E // CYCLE) as i:
                for r in range(CYCLE):
                    expert(pe.snap(CYCLE * i + r), UNITS * r % PLACES)
            for e in range(E - E % CYCLE, E):
                expert(e, UNITS * e % PLACES)
            total = pe.value_load(first_block[0:1, E:E + 1], min_val=1, max_val=BLOCKS)
            for t in range(TT):
                combine(total, t, last_comb[t])

        @block.scalar
        def _(act):
            act.wait_ge(consts_in, 48)
            act.activation(csig, c_sb, ACT.Sigmoid).then_inc(csig_ready, 1)
            for t in range(TA):
                if t == 0:
                    act.wait_ge(x_in, 16)
                if t == TT:
                    act.wait_ge(ctx_in, 16)
                src = x_sb[:, t, :] if t < TT else ctx_sb[:, t - TT, :]
                if t > 0:
                    act.wait_ge(squares, t)
                act.activation(square, src, ACT.Square, accum_out=ss[:, t:t + 1]).then_inc(squares, 1)

            def deviation(n, lo, hi):
                act.wait_ge(vars_ready, n)
                act.activation(std[:, lo:hi], var[:, lo:hi], ACT.Sqrt).then_inc(std_ready, 1)

            deviation(1, 0, TA)
            for k in range(1, KC, 2):
                act.wait_ge(xT_ps, k + 1)
                act.copy(hT[:, k, :], psum[:, k % 4, :]).then_inc(xT_act, 1)
            act.wait_ge(xT_act, KC // 2)
            act.wait_ge(a1_ready, 2)
            for v in range(2):
                for k in range(1, KC, 2):
                    half = hT[:, k, v * SEQ:(v + 1) * SEQ]
                    act.activation(half, half, ACT.Identity, bias=ada[:, k, v:v + 1],
                                   scale=a1[:, k, v:v + 1]).then_inc(hT_act, 1)
            def take_group(n):
                part, i = n // 8, n % 8
                act.wait_ge(proj_ps, n + 1)
                if part == 0:
                    ins = act.activation(qT[:, i, :], psum[:, n % 4, 0:SEQ], ACT.Copy, scale=HD ** -0.5)
                elif part == 1:
                    ins = act.copy(kT[:, i, :], psum[:, n % 4, :])
                else:
                    ins = act.copy(v_sb[:, i % 4, (i // 4) * BANK:(i // 4 + 1) * BANK], psum[:, n % 4, :])
                ins.then_inc(proj_sb, 1)

            def split_high(s):
                if s % 4 == 0:
                    act.wait_ge(qkv_in[2 + s // 4], 16)
                if s in range(4, STEPS // 2) or s >= 3 * STEPS // 4:
                    last = s - 4
                    if last % 4 == 3:
                        act.wait_ge(proj_ps, 8 + last + 1)
                    else:
                        act.wait_ge(w_used, 3 * (last // 4) + last % 4 + 1)
                act.copy(w_hi(s), w_raw(s)).then_inc(w_hi_ready, 1)

            for n in range(8):
                take_group(n)
                if n == 3:
                    act.wait_ge(hT_dve, KC)
                    act.wait_ge(hT_act, KC)
                    for k in range(KC):
                        act.copy(hT_hi_r[:, k, :], hT[:, k, :]).then_inc(hT_hi_ready, 1)
                if n == 5:
                    for s in range(4):
                        split_high(s)
            for blk in range(4):
                for i in range(3):
                    if blk < 3:
                        split_high(4 * (blk + 1) + i)
                for j in range(4):
                    take_group(8 + 4 * blk + j)
                if blk < 3:
                    split_high(4 * (blk + 1) + 3)

            def take_heads(j):
                act.wait_ge(pv_ps, j + 1)
                act.copy(oT[:, j, :], psum[:, 6 + j % 2, 0:SEQ]).then_inc(oT_ready, 1)

            for h in range(HEADS):
                act.wait_ge(negmax_ready, h + 1)
                if h < 2:
                    act.wait_ge(rows_ready, 4)
                else:
                    act.wait_ge(probsT_ps, h - 1)
                for t in range(TT):
                    act.activation(probs[h % 2][:, t, :], psum[:, 2 * (h % 2) + t, :], ACT.Exp,
                                   bias=negmax[:, h, t:t + 1],
                                   accum_out=psumexp[:, h, t:t + 1]).then_inc(probs_ready, 1)
                if h >= 3 and h % 2 == 1:
                    take_heads((h - 3) // 2)
            take_heads(KC - 1)
            def turned_input(t):
                act.wait_ge(h2T_ps, 2 * t + 2)
                act.copy(h2T[:, 4:8, t * P:(t + 1) * P],
                         psum[:, 2 * t + 1, :].rearrange("p (k n) -> p k n", k=4)).then_inc(h2T_act, 1)

            for t in range(TT):
                act.wait_ge(attn_out_ps, t + 1)
                act.wait_ge(squares, TA + 2 * t)
                act.activation(square, psum[:, 4 + 2 * t:6 + 2 * t, :].rearrange("p b n -> p (b n)"), ACT.Square,
                               accum_out=ss[:, 4 + t:5 + t]).then_inc(squares, 1)
                deviation(2 + 2 * t, 4 + t, 5 + t)
                if t == 1:
                    turned_input(0)
                act.wait_ge(x1_ready, t + 1)
                act.wait_ge(squares, TA + 2 * t + 1)
                act.activation(square, x_sb[:, t, :], ACT.Square, accum_out=ss[:, 6 + t:7 + t]).then_inc(squares, 1)
                deviation(3 + 2 * t, 6 + t, 7 + t)
            turned_input(1)
            act.wait_ge(route, 1)
            for t in range(TT):
                act.activation(e4[:, t, :], top8[:, t, 0:TOPK], ACT.Exp, bias=ntop[:, t:t + 1],
                               accum_out=e4s[:, t:t + 1]).then_inc(top_exp, 1)

            act.wait_ge(blocks_ready, 1)
            act.wait_ge(bdown_ps, 1)
            for t in range(TT):
                act.copy(acc[:, t, :], psum[:, COMB + 2 * t:COMB + 2 * t + 2, :].rearrange("p b n -> p (b n)")) \
                    .then_inc(comb_taken, 1)

            turned = turn_at.rearrange("p (c q s) -> p c q s", c=PC, q=PARTS)
            with act.Fori(0, E) as e:
                g_first = act.value_load(first_block[0:1, bass.ds(e, 1)], min_val=0, max_val=BLOCKS)
                g_end = act.value_load(first_block[0:1, bass.ds(e + 1, 1)], min_val=1, max_val=BLOCKS)
                with act.Fori(g_first, g_end) as g:
                    act.wait_ge(xg_ps, g + 1)
                    act.copy(xg_sb, xg_at).then_inc(xg_sb_ready, 1)
                    act.wait_ge(xgT_ps, g + 1)
                    act.copy(xgT, turned).then_inc(xgT_sb, 1)
                    act.wait_ge(swiglu, 4 * g + 1)
                    act.activation(sig_sb, gate_sb, ACT.Sigmoid, scale=ALPHA).then_inc(sig_ready, 1)
                    act.wait_ge(hidT_ps, g + 1)
                    act.copy(hidT, turned).then_inc(hidT_sb, 1)
                    act.wait_ge(y_ps, g + 1)
                    act.copy(y_sb, y_at).then_inc(y_ready, 1)
            for t in range(TT):
                act.wait_ge(fin_step, t + 1)
                act.wait_ge(squares, TA + 4 + t)
                act.activation(h2[:, t, :], acc[:, t, :], ACT.Square, accum_out=ss[:, 8 + t:9 + t]).then_inc(squares, 1)
                deviation(6 + t, 8 + t, 9 + t)

        @block.vector
        def _(dve):
            def inverse_deviation(n, n_squares, lo, hi):
                dve.wait_ge(squares, n_squares)
                dve.tensor_scalar(var[:, lo:hi], ss[:, lo:hi], 1.0 / D, EPS, ALU.mult, ALU.add).then_inc(vars_ready, 1)
                dve.wait_ge(std_ready, n)
                dve.reciprocal(rstd[:, lo:hi], std[:, lo:hi]).then_inc(rstd_ready, 1)
                dve.wait_ge(rstd_ready, n)

            dve.memset(silu, 0.0).then_inc(silu_ready, 1)
            dve.wait_ge(csig_ready, 1)
            dve.wait_ge(silu_ready, 1)
            dve.tensor_tensor(silu[:, :, 0:2], c_sb, csig, ALU.mult).then_inc(silu_ready, 1)
            inverse_deviation(1, TA, 0, TA)
            for t in range(TA):
                src = x_sb[:, t, :] if t < TT else ctx_sb[:, t - TT, :]
                dve.tensor_scalar(xn[:, t, :], src, rstd[:, t:t + 1], None, ALU.mult).then_inc(xn_ready, 1)

            def take_tokens(k):
                dve.wait_ge(xT_ps, k + 1)
                dve.tensor_copy(hT[:, k, :], psum[:, k % 4, :]).then_inc(xT_dve, 1)

            for k in range(0, KC - 2, 2):
                take_tokens(k)
            dve.wait_ge(ada_used, KC)
            dve.tensor_copy(ada_rows, psum[:, 4, :]).then_inc(ada_rows_sb, 1)
            take_tokens(KC - 2)
            dve.wait_ge(adaT_ps, 1)
            adaT = psum[:, 5, :].rearrange("p (c b v) -> p b c v", c=4, b=4)[:, :, :, 0:2]
            dve.tensor_tensor(ada.rearrange("p (b c) v -> p b c v", b=4), adaT,
                              bac.rearrange("p (b c) -> p b c", b=4).unsqueeze(3).to_broadcast([P, 4, 4, 2]),
                              ALU.add).then_inc(a1_ready, 1)
            dve.wait_ge(a1_ready, 1)
            dve.scalar_tensor_tensor(out=a1, in0=ada[:, KC:2 * KC, :], scalar=1.0,
                                     in1=ng0.unsqueeze(2).to_broadcast([P, KC, 2]),
                                     op0=ALU.add, op1=ALU.mult).then_inc(a1_ready, 1)
            dve.wait_ge(a1_ready, 2)
            dve.wait_ge(xT_dve, KC // 2)
            for v in range(2):
                for k in range(0, KC, 2):
                    half = hT[:, k, v * SEQ:(v + 1) * SEQ]
                    dve.tensor_scalar(half, half, a1[:, k, v:v + 1], ada[:, k, v:v + 1],
                                      ALU.mult, ALU.add).then_inc(hT_dve, 1)
            def split_low(s):
                dve.wait_ge(w_hi_ready, s + 1)
                dve.tensor_tensor(w_raw(s, w_lo_r), w_raw(s), w_hi(s).bitcast(F32),
                                  ALU.subtract).then_inc(w_lo_ready, 1)

            def low_tokens():
                dve.wait_ge(proj_ps, 8)
                for k in range(KC):
                    dve.wait_ge(hT_hi_ready, k + 1)
                    dve.tensor_tensor(hT_lo_r[:, k, :], hT[:, k, :], hT_hi_r[:, k, :].bitcast(F32),
                                      ALU.subtract).then_inc(hT_lo_ready, 1)

            step = 0
            for cb in range(4):
                for k in range(KC):
                    for s in SPLITS_AT.get((cb, k), ()):
                        split_low(s)
                    if (cb, k) == (0, 6):
                        low_tokens()
                    i = cb * KC + k
                    dve.wait_ge(ring_in[i % RING], 16 * (i // RING + 1))
                    if k == 0:
                        if cb >= 1:
                            dve.wait_ge(ada_sum_ps, cb)
                        ins = dve.tensor_scalar(ada_acc, ring[i % RING], silu[:, k, 0:1], None, ALU.mult)
                    else:
                        dve.wait_ge(ada_step, step)
                        ins = dve.scalar_tensor_tensor(out=ada_acc, in0=ring[i % RING], scalar=silu[:, k, 0:1],
                                                       in1=ada_acc, op0=ALU.mult, op1=ALU.add)
                    ins.then_inc(ada_step, 1)
                    step += 1
                if cb == 0:
                    dve.wait_ge(bada_in, 64)
                dve.wait_ge(ada_step, step)
                one = ada_acc[32 * cb:32 * cb + 1, :]
                dve.tensor_tensor(one, one, bada_rows[32 * cb:32 * cb + 1, :], ALU.add).then_inc(ada_step, 1)
                step += 1
                dve.wait_ge(ada_sum_ps, cb + 1)
                total = psum[:, 6:8, :].rearrange("p b n -> p (b n)")
                if cb == 0:
                    dve.wait_ge(rows_in, 48)
                    ins = dve.tensor_tensor(g1_row, total, g1_row, ALU.mult)
                elif cb == 1:
                    ins = dve.tensor_copy(sh2_row, total)
                elif cb == 2:
                    ins = dve.scalar_tensor_tensor(out=a2_row, in0=total, scalar=1.0, in1=a2_row,
                                                   op0=ALU.add, op1=ALU.mult)
                else:
                    ins = dve.tensor_tensor(g2_row[:], total, g2_row[:], ALU.mult)
                ins.then_inc(rows_ready, 1)
            for s in range(12, STEPS):
                split_low(s)

            for i in range(HEADS + 1):
                if i >= 1:
                    h = i - 1
                    dve.wait_ge(probs_ready, 2 * (h + 1))
                    dve.reciprocal(rsum[:, h, :], psumexp[:, h, :]).then_inc(rsum_ready, 1)
                    dve.wait_ge(rsum_ready, h + 1)
                    for t in range(TT):
                        ins = dve.tensor_scalar(probs[h % 2][:, t, :], probs[h % 2][:, t, :], rsum[:, h, t:t + 1],
                                                None, ALU.mult)
                    ins.then_inc(norm_ready, 1)
                if i < HEADS:
                    h = i
                    dve.wait_ge(scores_ps, h + 1)
                    dve.tensor_reduce(negmax[:, h, :], psum[:, 2 * (h % 2):2 * (h % 2) + 2, :], AX.X, ALU.max,
                                      negate=True).then_inc(negmax_ready, 1)
                if i >= 1:
                    h = i - 1
                    dve.wait_ge(probsT_ps, h + 1)
                    if h >= 2:
                        dve.wait_ge(pv_ps, h // 2)
                    dve.tensor_copy(probsT[h % 2].rearrange("p k n -> p (k n)"),
                                    psum[:, 4:6, :].rearrange("p b n -> p (b n)")).then_inc(probsT_sb, 1)
            def turned_input(t):
                dve.wait_ge(h2T_ps, 2 * t + 1)
                dve.tensor_copy(h2T[:, 0:4, t * P:(t + 1) * P],
                                psum[:, 2 * t, :].rearrange("p (k n) -> p k n", k=4)).then_inc(h2T_dve, 1)

            for t in range(TT):
                inverse_deviation(2 + 2 * t, TA + 2 * t + 1, 4 + t, 5 + t)
                dve.scalar_tensor_tensor(out=scaled[:, t, :], in0=psum[:, 4 + 2 * t:6 + 2 * t, :].rearrange("p b n -> p (b n)"),
                                         scalar=rstd[:, 4 + t:5 + t], in1=g1_row, op0=ALU.mult,
                                         op1=ALU.mult).then_inc(res_step, 1)
                dve.wait_ge(res_step, 2 * t + 1)
                dve.tensor_tensor(x_sb[:, t, :], scaled[:, t, :], x_sb[:, t, :], ALU.add).then_inc(x1_ready, 1)
                if t == 1:
                    turned_input(0)
                inverse_deviation(3 + 2 * t, TA + 2 * t + 2, 6 + t, 7 + t)
                if t == 0:
                    dve.wait_ge(bgu_step, 6)
                dve.wait_ge(x1_ready, t + 1)
                dve.scalar_tensor_tensor(out=scaled[:, t, :], in0=x_sb[:, t, :], scalar=rstd[:, 6 + t:7 + t],
                                         in1=a2_row, op0=ALU.mult, op1=ALU.mult).then_inc(res_step, 1)
                dve.wait_ge(res_step, 2 * t + 2)
                dve.tensor_tensor(h2[:, t, :], scaled[:, t, :], sh2_row, ALU.add).then_inc(h2_ready, 1)
            turned_input(1)

            steps = [1]

            def routed(ins):
                steps[0] += 1
                ins.then_inc(route_step, 1)
                dve.wait_ge(route_step, steps[0] - 1)

            dve.wait_ge(logits_ps, 1)
            dve.wait_ge(tables_in, 32)
            routed(dve.tensor_tensor(logits, psum[:, 4, 0:TT * E].rearrange("p (t e) -> p t e", t=TT),
                                     br_sb.unsqueeze(1).to_broadcast([P, TT, E]), ALU.add))
            for t in range(TT):
                routed(dve.max(top8[:, t, :], logits[:, t, :]))
                routed(dve.max_index(idx8[:, t, :], top8[:, t, :], logits[:, t, :]))
            dve.tensor_scalar(ntop[:], top8[:, :, 0], -1.0, None, ALU.mult).then_inc(route, 1)
            routed(dve.tensor_copy(idxf[:], idx8[:]))
            for t in range(TT):
                routed(dve.tensor_tensor(eq[:, t], slot_no[:, 0:E].unsqueeze(1).to_broadcast([P, TOPK, E]),
                                         idxf[:, t, 0:TOPK].unsqueeze(2).to_broadcast([P, TOPK, E]), ALU.is_equal))
                dve.tensor_reduce(member[:, t, :], eq[:, t].rearrange("p k e -> p e k"), AX.X,
                                  ALU.add).then_inc(member_ready, 1)
            dve.wait_ge(top_exp, TT)
            routed(dve.reciprocal(e4r[:], e4s[:]))
            routed(dve.tensor_tensor(g4[:], e4[:], e4r[:].unsqueeze(2).to_broadcast([P, TT, TOPK]), ALU.mult))
            for t in range(TT):
                routed(dve.tensor_tensor(geq[:, t], eq[:, t], g4[:, t, :].unsqueeze(2).to_broadcast([P, TOPK, E]),
                                         ALU.mult))
                dve.tensor_reduce(gates[:, t, :], geq[:, t].rearrange("p k e -> p e k"), AX.X,
                                  ALU.add).then_inc(gates_ready, 1)
            dve.wait_ge(pos_ps, 1)
            dve.wait_ge(member_ready, TT)
            routed(dve.scalar_tensor_tensor(out=pos[:], in0=psum[:, 5, 0:TT * E].rearrange("p (t e) -> p t e", t=TT),
                                            scalar=1.0, in1=member, op0=ALU.add, op1=ALU.mult))
            routed(dve.tensor_scalar(pos[:], pos[:], -1.0, None, ALU.add))
            counts = psum[0:1, 5, 2 * E:3 * E]
            begun = geq[0:1].rearrange("p t k e -> p (t k e)").rearrange("p (e n) -> p e n", e=E)
            routed(dve.tensor_tensor(begun, counts.unsqueeze(2).to_broadcast([1, E, SEQ // SLOTS]),
                                     slot_no[0:1, 0:SEQ:SLOTS].unsqueeze(1).to_broadcast([1, E, SEQ // SLOTS]),
                                     ALU.is_gt))
            routed(dve.tensor_reduce(nblk[:], begun, AX.X, ALU.add))
            routed(dve.tensor_scalar(nblk[:], nblk[:], 1.0, None, ALU.max))
            routed(dve.memset(one_row[:], 1.0))
            routed(dve.memset(cum[:, 0:1], 0.0))
            routed(dve.tensor_tensor_scan(cum[:, 1:E + 1], one_row[:], nblk[:], 0.0, ALU.mult, ALU.add))
            routed(dve.tensor_copy(first_block[:], cum[:]))
            dve.wait_ge(gatesT_ps, 1)
            dve.tensor_copy(gatesT, psum[0:E, 6, 0:SEQ]).then_inc(gatesT_sb, 1)
            dve.memset(y_sb, 0.0).then_inc(y_ready, 1)
            dve.memset(selT, 0.0).then_inc(selT_sb, 1)
            dve.memset(one_row[:], 1.0).then_inc(units_used, COUNTED)
            dve.wait_ge(selT_sb, 1)
            dve.wait_ge(y_ready, 1)
            dve.wait_ge(route_step, steps[0] - 1)
            dve.memset(cum[:, 0:1], 0.0).then_inc(blocks_ready, 1)

            def add_rows(g, t, bank=COMB):
                a = acc[:, t, :].rearrange("p (q n) -> p q n", q=PARTS)
                dve.wait_ge(comb_ps, 2 * g + t + 1)
                dve.wait_ge(comb_taken, 2 * g + t + 1)
                dve.tensor_tensor(a, psum[:, bank:bank + PARTS, 0:PW], a, ALU.add) \
                    .then_inc(comb_taken, 1)

            with dve.Fori(0, E) as e:
                g_first = dve.value_load(first_block[0:1, bass.ds(e, 1)], min_val=0, max_val=BLOCKS)
                g_end = dve.value_load(first_block[0:1, bass.ds(e + 1, 1)], min_val=1, max_val=BLOCKS)
                with dve.Fori(g_first, g_end) as g:
                    j0 = nc.s_assert_within((g - g_first) * SLOTS, 0, SEQ - SLOTS,
                                            skip_runtime_bounds_check_because="an expert has at most SEQ / SLOTS blocks")
                    for t in range(TT):
                        dve.tensor_scalar(sel[:, t, :], slot_no[:, bass.ds(j0, SLOTS)], pos[:, t, bass.ds(e, 1)],
                                          None, ALU.is_equal)
                        dve.tensor_scalar(sel_gate[:, t], slot_no[:, bass.ds(j0, SLOTS)].unsqueeze(1)
                                          .to_broadcast([P, PARTS, SLOTS]), pos[:, t, bass.ds(e, 1)],
                                          gates[:, t, bass.ds(e, 1)], ALU.is_equal, ALU.mult)
                    dve.tensor_scalar(pick[:], expert_no[:].to_broadcast([3 * E, SLOTS]),
                                      slot_no[0:3 * E, bass.ds(e, 1)], None, ALU.is_equal).then_inc(sel_ready, 1)
                    add_rows(g, 0)
                    dve.wait_ge(gu_ps, g + 1)
                    dve.tensor_scalar(gate_sb, psum[:, GATE_UP, 0:PW], LIMIT, None, ALU.min).then_inc(swiglu, 1)
                    dve.tensor_scalar(up_sb, psum[:, GATE_UP, PW:2 * PW], LIMIT, -LIMIT, ALU.min, ALU.max).then_inc(swiglu, 1)
                    dve.wait_ge(sig_ready, g + 1)
                    dve.tensor_tensor(sig_sb, gate_sb, sig_sb, ALU.mult).then_inc(swiglu, 1)
                    dve.wait_ge(swiglu, 4 * g + 3)
                    dve.scalar_tensor_tensor(out=hid_sb, in0=up_sb, scalar=1.0, in1=sig_sb,
                                             op0=ALU.add, op1=ALU.mult).then_inc(swiglu, 1)
                    add_rows(g, 1)
                    dve.wait_ge(selT_ps, g + 1)
                    dve.tensor_copy(selT, selT_at).then_inc(selT_sb, 1)
            total = dve.value_load(first_block[0:1, E:E + 1], min_val=1, max_val=BLOCKS)
            for t in range(TT):
                add_rows(total, t, last_comb[t])
                dve.wait_ge(comb_taken, 2 * total + 3 + t)
                dve.memset(ntop[:, t:t + 1], 0.0).then_inc(fin_step, 1)
            for t in range(TT):
                inverse_deviation(6 + t, TA + 5 + t, 8 + t, 9 + t)
                dve.scalar_tensor_tensor(out=acc[:, t, :], in0=acc[:, t, :], scalar=rstd[:, 8 + t:9 + t],
                                         in1=g2_row[:], op0=ALU.mult, op1=ALU.mult).then_inc(fin_step, 1)
                dve.wait_ge(fin_step, TT + t + 1)
                dve.tensor_tensor(h2[:, t, :], acc[:, t, :], x_sb[:, t, :], ALU.add).then_inc(fin_ready, 1)


def kernel(**inputs):
    import numpy as np
    import concourse.bacc as bacc
    from concourse.bass_utils import run_bass_kernel_spmd as run

    a = {n: np.asarray(v) for n, v in inputs.items()}

    def cols(v):
        return np.ascontiguousarray(np.moveaxis(v.reshape(v.shape[:-1] + (-1, P)), -1, 0))

    host = {
        "x": a["x"],
        "c_cols": np.ascontiguousarray(np.stack([cols(a["c"][0]), cols(a["c_ctx"])], axis=-1)),
        "ctx": a["ctx"],
        "w_ada": a["w_ada"],
        "b_ada_cols": cols(a["b_ada"][0, 0:2 * D]),
        "b_ada": a["b_ada"],
        "norm_cols": cols(a["norm_g"][0, 0]),
        "norm_g": a["norm_g"],
        "w_qkv": a["w_qkv"],
        "w_o": a["w_o"],
        "rpb": a["rpb"],
        "w_router": a["w_router"],
        "b_router": a["b_router"],
        "w_gu": a["w_gu"][0],
        "b_gu": a["b_gu"][0],
        "w_down": a["w_down"][0],
        "b_down": a["b_down"],
    }
    nc = bacc.Bacc("TRN2", target_bir_lowering=False, num_devices=1)
    arrays, args = {}, []
    for name, v in host.items():
        arrays[f"in_{name}"] = np.ascontiguousarray(v)
        args.append(nc.dram_tensor(f"in_{name}", v.shape, F32, kind="ExternalInput").ap())
    out = nc.dram_tensor("out_0", (1, SEQ, D), F32, kind="ExternalOutput").ap()
    build(nc, *args, out)
    r = run(nc, [arrays], core_ids=[0])
    return r.results[0]["out_0"]
```
